# Optimizing a Trainium2 kernel written in Bass

```python
import jax, jax.numpy as jnp
from jax import lax
import numpy as np

D_MODEL = 1024
BATCH = 1
SEQ = 256
DEPTH = 2

CHUNK = 64
Q_BLOCK = 128
D_FF = 2816
C_CONV = 512
CONV_WIDTH = 31
N_HEADS = 8
NOPE_DIM = 64
ROPE_DIM = 32
QK_DIM = NOPE_DIM + ROPE_DIM
V_DIM = 64
Q_LORA = 256
KV_LORA = 256
ROPE_THETA = 10000.0
EPS = 1e-6
D_IN = 2 * C_CONV + Q_LORA + KV_LORA + ROPE_DIM + 2 * D_MODEL

kernel_name = 'hybrid_conformer_mla_gated'

def _rms_norm(x, g):
    x32 = x.astype(jnp.float32)
    y = x32 * lax.rsqrt(jnp.mean(x32 * x32, axis=-1, keepdims=True) + EPS)
    return (y * g.astype(jnp.float32)).astype(x.dtype)

def _layer_norm(x, g, b):
    x32 = x.astype(jnp.float32)
    mu = jnp.mean(x32, axis=-1, keepdims=True)
    xc = x32 - mu
    y = xc * lax.rsqrt(jnp.mean(xc * xc, axis=-1, keepdims=True) + EPS)
    return (y * g.astype(jnp.float32) + b.astype(jnp.float32)).astype(x.dtype)

def _swiglu(h, w_gate, w_up, w_down):
    return (jax.nn.silu(h @ w_gate) * (h @ w_up)) @ w_down

def _rope(x, cos, sin):
    x1, x2 = jnp.split(x.astype(jnp.float32), 2, axis=-1)
    return jnp.concatenate([x1 * cos - x2 * sin, x2 * cos + x1 * sin], axis=-1).astype(x.dtype)

def _conv_module(u2, conv_w, conv_b, ln_g, ln_b, w_conv_out):
    a, gate = jnp.split(u2, 2, axis=-1)
    u = a * jax.nn.sigmoid(gate)
    u = lax.conv_general_dilated(
        u, conv_w[:, None, :], window_strides=(1,), padding=[(CONV_WIDTH - 1, 0)],
        dimension_numbers=('NWC', 'WIO', 'NWC'), feature_group_count=C_CONV) + conv_b
    u = jax.nn.silu(_layer_norm(u, ln_g, ln_b))
    return u @ w_conv_out

def _chunk_causal_attention(q, k, v):
    b, s, h, dq = q.shape
    nb = s // Q_BLOCK
    scale = dq ** -0.5
    key_chunk = jnp.arange(s) // CHUNK
    q_blocks = q.reshape(b, nb, Q_BLOCK, h, dq).transpose(1, 0, 2, 3, 4)

    def one_block(args):
        qi, i = args
        scores = jnp.einsum('bqhd,bkhd->bhqk', qi, k).astype(jnp.float32) * scale
        q_chunk = (i * Q_BLOCK + jnp.arange(Q_BLOCK)) // CHUNK
        mask = key_chunk[None, :] <= q_chunk[:, None]
        p = jax.nn.softmax(jnp.where(mask, scores, -jnp.inf), axis=-1)
        return jnp.einsum('bhqk,bkhd->bqhd', p.astype(v.dtype), v)

    out = lax.map(one_block, (q_blocks, jnp.arange(nb)))
    return out.transpose(1, 0, 2, 3, 4).reshape(b, s, h, v.shape[-1])

def _mla(c_q, c_kv, k_rope, cos, sin, cq_norm, ckv_norm, w_uq, w_ukv, q_norm, k_norm, w_mla_out):
    b, s, _ = c_q.shape
    q = (_rms_norm(c_q, cq_norm) @ w_uq).reshape(b, s, N_HEADS, QK_DIM)
    kv = (_rms_norm(c_kv, ckv_norm) @ w_ukv).reshape(b, s, N_HEADS, NOPE_DIM + V_DIM)
    k_nope, v = kv[..., :NOPE_DIM], kv[..., NOPE_DIM:]
    k_r = jnp.broadcast_to(k_rope[:, :, None, :], (b, s, N_HEADS, ROPE_DIM))
    k = jnp.concatenate([k_nope, k_r], axis=-1)
    q = _rms_norm(q, q_norm)
    k = _rms_norm(k, k_norm)
    q = jnp.concatenate([q[..., :NOPE_DIM], _rope(q[..., NOPE_DIM:], cos, sin)], axis=-1)
    k = jnp.concatenate([k[..., :NOPE_DIM], _rope(k[..., NOPE_DIM:], cos, sin)], axis=-1)
    o = _chunk_causal_attention(q, k, v)
    return o.reshape(b, s, N_HEADS * V_DIM) @ w_mla_out

def setup_inputs(seed: int = 0) -> dict:
    key = jax.random.key(seed)
    ks = jax.random.split(key, 32)

    def nrm(k, shape, fan_in):
        return jax.random.normal(k, shape, jnp.float32) * fan_in ** -0.5

    def gain(k, shape):
        return 1.0 + 0.05 * jax.random.normal(k, shape, jnp.float32)

    def small(k, shape, s):
        return s * jax.random.normal(k, shape, jnp.float32)

    x = jax.random.normal(ks[0], (BATCH, SEQ, D_MODEL), jnp.float32)
    offset = jax.random.randint(ks[1], (BATCH, 1), 0, 1024, dtype=jnp.int32)
    positions = offset + jnp.arange(SEQ, dtype=jnp.int32)[None, :]
    return {
        'x': x,
        'positions': positions,
        'ffn1_norm': gain(ks[2], (DEPTH, D_MODEL)),
        'ffn1_w_gate': nrm(ks[3], (DEPTH, D_MODEL, D_FF), D_MODEL),
        'ffn1_w_up': nrm(ks[4], (DEPTH, D_MODEL, D_FF), D_MODEL),
        'ffn1_w_down': nrm(ks[5], (DEPTH, D_FF, D_MODEL), D_FF),
        'mix_norm': gain(ks[6], (DEPTH, D_MODEL)),
        'w_in': nrm(ks[7], (DEPTH, D_MODEL, D_IN), D_MODEL),
        'gate_bias': small(ks[8], (DEPTH, 2, D_MODEL), 0.1),
        'conv_w': nrm(ks[9], (DEPTH, CONV_WIDTH, C_CONV), CONV_WIDTH),
        'conv_b': small(ks[10], (DEPTH, C_CONV), 0.02),
        'conv_ln_g': gain(ks[11], (DEPTH, C_CONV)),
        'conv_ln_b': small(ks[12], (DEPTH, C_CONV), 0.02),
        'w_conv_out': nrm(ks[13], (DEPTH, C_CONV, D_MODEL), C_CONV),
        'cq_norm': gain(ks[14], (DEPTH, Q_LORA)),
        'ckv_norm': gain(ks[15], (DEPTH, KV_LORA)),
        'w_uq': nrm(ks[16], (DEPTH, Q_LORA, N_HEADS * QK_DIM), Q_LORA),
        'w_ukv': nrm(ks[17], (DEPTH, KV_LORA, N_HEADS * (NOPE_DIM + V_DIM)), KV_LORA),
        'q_norm': gain(ks[18], (DEPTH, QK_DIM)),
        'k_norm': gain(ks[19], (DEPTH, QK_DIM)),
        'w_mla_out': nrm(ks[20], (DEPTH, N_HEADS * V_DIM, D_MODEL), N_HEADS * V_DIM),
        'w_out': nrm(ks[21], (DEPTH, D_MODEL, D_MODEL), D_MODEL),
        'ffn2_norm': gain(ks[22], (DEPTH, D_MODEL)),
        'ffn2_w_gate': nrm(ks[23], (DEPTH, D_MODEL, D_FF), D_MODEL),
        'ffn2_w_up': nrm(ks[24], (DEPTH, D_MODEL, D_FF), D_MODEL),
        'ffn2_w_down': nrm(ks[25], (DEPTH, D_FF, D_MODEL), D_FF),
    }

def reference(x, positions, ffn1_norm, ffn1_w_gate, ffn1_w_up, ffn1_w_down, mix_norm, w_in,
              gate_bias, conv_w, conv_b, conv_ln_g, conv_ln_b, w_conv_out, cq_norm, ckv_norm,
              w_uq, w_ukv, q_norm, k_norm, w_mla_out, w_out, ffn2_norm, ffn2_w_gate, ffn2_w_up,
              ffn2_w_down):
    b, s, _ = x.shape
    inv_freq = ROPE_THETA ** (-jnp.arange(0, ROPE_DIM, 2, dtype=jnp.float32) / ROPE_DIM)
    ang = positions.astype(jnp.float32)[..., None] * inv_freq
    cos = jnp.cos(ang)[:, :, None, :]
    sin = jnp.sin(ang)[:, :, None, :]
    o1 = 2 * C_CONV
    o2 = o1 + Q_LORA
    o3 = o2 + KV_LORA
    o4 = o3 + ROPE_DIM
    for l in range(DEPTH):
        x = x + 0.5 * _swiglu(_rms_norm(x, ffn1_norm[l]), ffn1_w_gate[l], ffn1_w_up[l], ffn1_w_down[l])
        h = _rms_norm(x, mix_norm[l])
        proj = h @ w_in[l]
        y_conv = _conv_module(proj[..., :o1], conv_w[l], conv_b[l], conv_ln_g[l], conv_ln_b[l],
                              w_conv_out[l])
        y_mla = _mla(proj[..., o1:o2], proj[..., o2:o3], proj[..., o3:o4], cos, sin,
                     cq_norm[l], ckv_norm[l], w_uq[l], w_ukv[l], q_norm[l], k_norm[l], w_mla_out[l])
        gates = jax.nn.sigmoid(proj[..., o4:].reshape(b, s, 2, D_MODEL) + gate_bias[l])
        y = gates[:, :, 0] * y_conv + gates[:, :, 1] * y_mla
        x = x + y @ w_out[l]
        x = x + 0.5 * _swiglu(_rms_norm(x, ffn2_norm[l]), ffn2_w_gate[l], ffn2_w_up[l], ffn2_w_down[l])
    return x


_drawn_inputs = setup_inputs


def setup_inputs(seed=0):
    import zlib

    import numpy as np

    out = dict(_drawn_inputs(seed))
    spreads = {}
    factors = {'gate_bias': 3.198,
     'conv_b': 2.993,
     'conv_ln_b': 6.404,
     'cq_norm': 8.0,
     'ckv_norm': 7.192,
     'q_norm': 8.0,
     'k_norm': 8.0}
    for name, (base, spread) in spreads.items():
        noise = np.random.default_rng([zlib.crc32(name.encode()), seed]).standard_normal(out[name].shape)
        drawn = base * np.exp(spread * noise) if base else spread * noise
        out[name] = __import__('jax').numpy.asarray(drawn.astype(out[name].dtype))
    for name, factor in factors.items():
        out[name] = (out[name] * factor).astype(out[name].dtype)
    return out
```

```python
from contextlib import ExitStack

import numpy as np

import concourse.bass as bass
from concourse import mybir

ALU = mybir.AluOpType
ACT = mybir.ActivationFunctionType
AX = mybir.AxisListType
F32 = mybir.dt.float32
F32R = mybir.dt.float32r
BF16 = mybir.dt.bfloat16
I32 = mybir.dt.int32

P = 128
DEPTH = 2
D = 1024
SEQ = 256
TT = SEQ // P
KD = D // P
F = 2816
FC = 256
NCH = F // FC
C = 512
CT = C // P
W = 31
H = 8
NOPE, ROPE, VD = 64, 32, 64
QK = NOPE + ROPE
HALF = ROPE // 2
QL = KVL = 256
PR = QL + KVL + ROPE
O1 = 2 * C
O4 = O1 + PR
CHUNK = 64
EPS = 1e-6
SCALE = float(QK) ** -0.5
MASKED = -1e30

UNIT = 4 * PR
RAW = 3
RING = 6
LEAD = 5
U_FFN = 3 * NCH
U_MIX = 24
U_LAYER = 2 * U_FFN + U_MIX
UB = (0, U_FFN + U_MIX)
UM = U_FFN
assert U_LAYER % RING == 0 and U_LAYER % RAW == 0

M_PR, M_C01, M_UQ, M_UKV, M_C23, M_G, M_MLA, M_CO, M_WO = 0, 2, 4, 5, 6, 8, 16, 18, 20

USED = [2048] * U_LAYER
USED[UM + M_PR] = USED[UM + M_PR + 1] = 4 * PR
USED[UM + M_UQ] = 2 * H * QK

N_TAP = CT * (W + 1)
N_ROPE = 24

V_W = 0
V_CB = CT * W
V_LG = V_CB + CT
V_LB = V_LG + CT
V_CQ = V_LB + CT
V_CKV = V_CQ + 2
V_N = V_CKV + 2


def unit_gu(f, c, h):
    if isinstance(c, int) and c == 0:
        return UB[f] + h
    return (c - 1) * 3 + (UB[f] + 2 + h)


def unit_down(f, c):
    if isinstance(c, int) and c == NCH - 1:
        return UB[f] + U_FFN - 1
    return c * 3 + (UB[f] + 4)


def two_pi_parts(value, quanta):
    parts = []
    for q in quanta:
        parts.append(float(np.floor(value / q) * q))
        value -= parts[-1]
    return parts + [float(np.float32(value))]


def trunk(nc, a):
    with ExitStack() as ctx:
        def sb(name, shape, dt=F32):
            return ctx.enter_context(nc.sbuf_tensor(name, shape, dt))

        def sem(name):
            return ctx.enter_context(nc.semaphore(name))

        raw = sb("raw", [P, RAW, UNIT])
        whi = sb("whi", [P, RING, UNIT], F32R)
        wlo = sb("wlo", [P, RING, UNIT], F32R)
        x = sb("x", [P, TT, D])
        hThi = sb("hThi", [P, KD, SEQ], F32R)
        hTlo = sb("hTlo", [P, KD, SEQ], F32R)
        gThi = sb("gThi", [P, 4, SEQ], F32R)
        gTlo = sb("gTlo", [P, 4, SEQ], F32R)
        htok = sb("htok", [P, TT * D])
        gain = sb("gain", [P, D])
        gates = sb("gates", [P, TT, 2 * D])
        ktok = sb("ktok", [P, TT, H, QK])
        vtok = sb("vtok", [P, TT, H, VD])
        cu = sb("cu", [P, CT, W - 1 + SEQ])
        cacc = sb("cacc", [P, CT, SEQ])
        qkT = sb("qkT", [P, 2, 2 * SEQ])
        pT = sb("pT", [P, 2, 3 * P])
        bias = sb("bias", [P, C])
        mask = sb("mask", [P, SEQ])
        ident = sb("ident", [P, P])
        mean_of = sb("mean_of", [P, P])
        vec = sb("vec", [P, V_N])
        qkg = sb("qkg", [P, 2, QK])
        posi = sb("posi", [P, TT], I32)
        ang = sb("ang", [P, 4, TT, HALF])
        cossin = sb("cossin", [P, 2, TT, HALF])
        small = sb("small", [P, 96])
        expo = sb("expo", [P, 1])
        zero = sb("zero", [P, C], BF16)

        ss = small[:, 0:2]
        ms = small[:, 2:4]
        rs = small[:, 4:6]
        ss4 = small[:, 6:10]
        rs4 = small[:, 10:14]
        ssqk = small[:, 14:46]
        rsqk = small[:, 46:78]
        mx = small[:, 78:80]
        nmx = small[:, 80:82]
        psum_h = small[:, 82:84]
        rsum = (small[:, 84:86], small[:, 86:88])
        sgate = gates[:, 0, 0:TT * FC].rearrange("p (t f) -> p t f", t=TT)
        gu = gates[:, 1, 0:TT * FC].rearrange("p (t f) -> p t f", t=TT)
        pr = gates[:, :, 2 * D - PR:2 * D]
        junk = gates[:, :, 0:H * QK]
        qtok = htok[:, 0:TT * H * QK].rearrange("p (t h d) -> p t h d", t=TT, h=H)
        otok = gain[:, :].rearrange("p (t n) -> p t n", t=TT)
        lnr = qkT[:, 0, 0:SEQ]
        tail = htok[:, TT * H * QK:TT * D]
        rot = tail.rearrange("p (j t h d) -> p j t h d", j=2, t=TT, h=H)
        prob = tail.rearrange("p (t k) -> p t k", t=TT)
        csq = cu[:, :, W - 1:W - 1 + SEQ]

        bank = ctx.enter_context(nc.psum_tensor("bank", [P, 8, 512], F32))

        raw_landed = [sem(f"raw_landed{i}") for i in range(RAW)]
        whi_ready = sem("whi_ready")
        wlo_ready = sem("wlo_ready")
        unit_free = sem("unit_free")
        small_landed = sem("small_landed")
        x_landed = sem("x_landed")
        gain_landed = sem("gain_landed")
        bias_landed = sem("bias_landed")
        vec_landed = sem("vec_landed")
        vec_used = sem("vec_used")
        const_ready = sem("const_ready")
        dve_const = sem("dve_const")
        rope_step = sem("rope_step")
        trig_ready = sem("trig_ready")
        x_new = sem("x_new")
        sq_ready = sem("sq_ready")
        ms_ready = sem("ms_ready")
        rs_ready = sem("rs_ready")
        h_ready = sem("h_ready")
        ntr = sem("ntr")
        nhi = sem("nhi")
        nlo = sem("nlo")
        gu_done = sem("gu_done")
        silu_ready = sem("silu_ready")
        gu_ready = sem("gu_ready")
        gtr = sem("gtr")
        ghi = sem("ghi")
        glo = sem("glo")
        acc_done = sem("acc_done")
        pr_done = sem("pr_done")
        pr_ready = sem("pr_ready")
        kr_ready = sem("kr_ready")
        pr_sq = sem("pr_sq")
        pr_ms = sem("pr_ms")
        pr_rs = sem("pr_rs")
        pr_norm = sem("pr_norm")
        lat_tr = sem("lat_tr")
        lat_hi = sem("lat_hi")
        lat_lo = sem("lat_lo")
        tanh_ready = sem("tanh_ready")
        cu_ready = sem("cu_ready")
        q_done = sem("q_done")
        kv_done = sem("kv_done")
        q_ready = sem("q_ready")
        kv_ready = sem("kv_ready")
        qk_sq = sem("qk_sq")
        qk_sum = sem("qk_sum")
        qk_ms = sem("qk_ms")
        qk_rs = sem("qk_rs")
        qk_norm = sem("qk_norm")
        pool_step = sem("pool_step")
        gate_done = sem("gate_done")
        gate_sum = sem("gate_sum")
        gate_ready = sem("gate_ready")
        qkt_done = sem("qkt_done")
        qkt_ready = sem("qkt_ready")
        s_done = sem("s_done")
        max_ready = sem("max_ready")
        nmx_ready = sem("nmx_ready")
        exp_ready = sem("exp_ready")
        rsum_ready = sem("rsum_ready")
        pt_done = sem("pt_done")
        pt_ready = sem("pt_ready")
        pv_done = sem("pv_done")
        o_ready = sem("o_ready")
        ot_done = sem("ot_done")
        ot_hi = sem("ot_hi")
        ot_lo = sem("ot_lo")
        tap = sem("tap")
        mean_done = sem("mean_done")
        xc_ready = sem("xc_ready")
        csq_ready = sem("csq_ready")
        var_done = sem("var_done")
        lnv_ready = sem("lnv_ready")
        lnr_ready = sem("lnr_ready")
        ln_ready = sem("ln_ready")
        act_silu = sem("act_silu")
        c_hi = sem("c_hi")
        c_lo = sem("c_lo")
        mla_done = sem("mla_done")
        ym_ready = sem("ym_ready")
        co_done = sem("co_done")
        yc_ready = sem("yc_ready")
        y_ready = sem("y_ready")
        yt_done = sem("yt_done")
        yt_hi = sem("yt_hi")
        yt_lo = sem("yt_lo")
        stored = sem("stored")

        wg = (a["ffn1_w_gate"], a["ffn2_w_gate"])
        wu = (a["ffn1_w_up"], a["ffn2_w_up"])
        wd = (a["ffn1_w_down"], a["ffn2_w_down"])
        norms = (a["ffn1_norm"], a["mix_norm"], a["ffn2_norm"])

        def unit_waits(eng, l, u):
            eng.wait_ge(wlo_ready, l * U_LAYER + u + (RAW + 1))

        def unit_released(eng, l, u):
            eng.wait_ge(unit_free, l * U_LAYER + u + (RING + 1))

        def per_ffn(l, f, c, t):
            return l * (4 * NCH) + c * TT + (2 * NCH * f + t + 1)

        def per_norm(l, n, t):
            return l * (3 * TT) + (n * TT + t + 1)

        def per_norm_half(l, n, t, h):
            return l * (6 * TT) + ((n * TT + t) * 2 + h + 1)

        def slot(u, n):
            return u % n

        def view(t, u0, n, k):
            return t[:, slot(u0, RING), 0:n].rearrange("p (k n) -> p k n", k=k)

        block = ctx.enter_context(nc.Block())

        def chunks(eng, f, first, pair, last):
            first()
            with eng.Fori(0, (NCH - 3) // 2) as i:
                pair(i * 2 + 1, 1)
                pair(i * 2 + 2, 2)
            last()

        @block.sync
        def _(sp):
            def place(l, u, u0, pairs):
                sp.wait_ge(wlo_ready, l * U_LAYER + u + 1)
                for dst, src in pairs:
                    sp.dma_start(dst, src).then_inc(raw_landed[slot(u0, RAW)], 16)

            def gate_up(l, f, c, c0, h):
                u0 = unit_gu(f, c0, h)
                dst = raw[:, slot(u0, RAW), 0:2048].rearrange("p (k g n) -> p k g n", k=4, g=2)
                rows = slice(4 * h * P, 4 * (h + 1) * P)
                cols = bass.ds(c * FC, FC)
                place(l, unit_gu(f, c, h), u0, [
                    (dst[:, :, g, :], w[l, rows, cols].rearrange("(k p) n -> p k n", p=P))
                    for g, w in enumerate((wg[f], wu[f]))])

            def down(l, f, c, c0):
                u0 = unit_down(f, c0)
                dst = raw[:, slot(u0, RAW), 0:2048].rearrange("p (k n) -> p k n", k=2)
                place(l, unit_down(f, c), u0, [
                    (dst[:, k, :], wd[f][l, bass.ds(c * FC + k * P, P), :]) for k in range(2)])

            def ffn(l, f):
                def first():
                    gate_up(l, f, 0, 0, 0)
                    gate_up(l, f, 0, 0, 1)

                def pair(c, c0):
                    gate_up(l, f, c, c0, 0)
                    gate_up(l, f, c, c0, 1)
                    down(l, f, c - 1, c0 - 1)

                def last():
                    for c in (NCH - 2, NCH - 1):
                        pair(c, c)
                    down(l, f, NCH - 1, NCH - 1)

                chunks(sp, f, first, pair, last)

            def block_of(l, u, w, r0, k, c0, n, split_cols=False):
                dst = raw[:, slot(u, RAW), 0:k * n].rearrange("p (k n) -> p k n", k=k)
                src = w[l, r0:r0 + k * P, c0:c0 + n].rearrange("(k p) n -> p k n", p=P)
                h = k // 2
                place(l, u, u, [(dst[:, h:k], src[:, h:k]), (dst[:, 0:h], src[:, 0:h])])

            def load_gain(l, n):
                sp.wait_ge(h_ready, l * (3 * TT) + (n * TT + 1))
                sp.dma_start(gain[:, :], norms[n][bass.ds(l, 1), :].to_broadcast([P, D])).then_inc(gain_landed, 16)

            sp.dma_start(x[:, 0, :], a["x"][0, 0:P, :]).then_inc(x_landed, 16)
            sp.dma_start(x[:, 1, :], a["x"][0, P:SEQ, :]).then_inc(x_landed, 16)
            for t in range(TT):
                sp.dma_start(posi[:, t:t + 1], a["positions"][0, t * P:(t + 1) * P].unsqueeze(1)).then_inc(small_landed, 16)

            with sp.Fori(0, DEPTH) as l:
                load_gain(l, 0)
                sp.wait_ge(vec_used, l + 1)
                sp.dma_start(vec[:, :], a["vec"][l]).then_inc(vec_landed, 16)
                for n, w in enumerate((a["q_norm"], a["k_norm"])):
                    sp.dma_start(qkg[:, n, :], w[bass.ds(l, 1), :].to_broadcast([P, QK])).then_inc(vec_landed, 16)
                ffn(l, 0)
                load_gain(l, 1)
                for h in range(2):
                    block_of(l, UM + M_PR + h, a["w_in"], 4 * h * P, 4, O1, PR)
                def conv_units(base, j):
                    for g in range(2):
                        block_of(l, UM + base + g, a["w_in"], 0, KD, g * C + j * 256, 256)

                conv_units(M_C01, 0)
                block_of(l, UM + M_UQ, a["w_uq"], 0, 2, 0, H * QK)
                block_of(l, UM + M_UKV, a["w_ukv"], 0, 2, 0, H * (NOPE + VD))
                conv_units(M_C23, 1)
                for g in range(4):
                    for h in range(2):
                        block_of(l, UM + M_G + 2 * g + h, a["w_in"], 4 * h * P, 4, O4 + g * C, C)
                for h in range(2):
                    block_of(l, UM + M_MLA + h, a["w_mla_out"], 2 * h * P, 2, 0, D)
                for h in range(2):
                    block_of(l, UM + M_CO + h, a["w_conv_out"], 2 * h * P, 2, 0, D)
                for h in range(4):
                    block_of(l, UM + M_WO + h, a["w_out"], 2 * h * P, 2, 0, D)
                ffn(l, 1)

            for t in range(TT):
                sp.wait_ge(x_new, TT + 6 * DEPTH - (TT - 1 - t))
                sp.dma_start(a["out"][0, t * P:(t + 1) * P, :], x[:, t, :]).then_inc(stored, 16)
            sp.wait_ge(gain_landed, 16 * 3 * DEPTH)
            sp.wait_ge(stored, 16 * TT)

        @block.gpsimd
        def _(pool):
            nc.gpsimd.memset(ident[:, :], 0.0).then_inc(const_ready, 1)
            nc.gpsimd.memset(expo[:, :], -0.5).then_inc(const_ready, 1)
            nc.gpsimd.memset(mean_of[:, :], 1.0 / C).then_inc(const_ready, 1)
            pool.wait_ge(const_ready, 3)
            nc.gpsimd.affine_select(out=ident[:, :], in_=ident[:, :], compare_op=ALU.not_equal, fill=1.0,
                                    base=0, pattern=[[-1, P]], channel_multiplier=1).then_inc(const_ready, 1)

            def root(out, in_):
                return nc.gpsimd.tensor_tensor(out, in_, expo[:, :].to_broadcast([P, out.shape[-1]]), ALU.pow)

            def norm(l, n):
                for t in range(TT):
                    pool.wait_ge(ms_ready, per_norm(l, n, t))
                    root(rs[:, t:t + 1], ms[:, t:t + 1]).then_inc(rs_ready, 1)

            with pool.Fori(0, DEPTH) as l:
                norm(l, 0)
                norm(l, 1)
                pool.wait_ge(pr_ms, l + 1)
                root(rs4, ss4).then_inc(pr_rs, 1)
                steps = 0
                for j, tok in enumerate((qtok, ktok[:, :, :, :])):
                    pool.wait_ge(qk_ms, l * 2 + j + 1)
                    root(rsqk[:, 16 * j:16 * j + 16], ssqk[:, 16 * j:16 * j + 16]).then_inc(qk_rs, 1)
                for j, tok in enumerate((qtok, ktok[:, :, :, :])):
                    pool.wait_ge(qk_norm, l * 2 + j + 1)
                    if j == 0:
                        pool.wait_ge(vec_landed, (l + 1) * 48)
                        pool.wait_ge(trig_ready, 2)

                    def step(ins):
                        nonlocal steps
                        steps += 1
                        ins.then_inc(pool_step, 1)

                    def seen():
                        pool.wait_ge(pool_step, l * 16 + steps)

                    for t in range(TT):
                        step(nc.gpsimd.tensor_tensor(tok[:, t], tok[:, t],
                                                     qkg[:, j:j + 1, :].to_broadcast([P, H, QK]), ALU.mult))
                    lo_half, hi_half = tok[:, :, :, NOPE:NOPE + HALF], tok[:, :, :, NOPE + HALF:QK]
                    cos, sin = (cossin[:, s].unsqueeze(2).to_broadcast([P, TT, H, HALF]) for s in range(2))
                    seen()
                    step(nc.gpsimd.tensor_tensor(rot[:, 0], hi_half, sin, ALU.mult))
                    step(nc.gpsimd.tensor_tensor(rot[:, 1], lo_half, sin, ALU.mult))
                    seen()
                    step(nc.gpsimd.tensor_tensor(lo_half, lo_half, cos, ALU.mult))
                    step(nc.gpsimd.tensor_tensor(hi_half, hi_half, cos, ALU.mult))
                    seen()
                    step(nc.gpsimd.tensor_tensor(lo_half, lo_half, rot[:, 0], ALU.subtract))
                    step(nc.gpsimd.tensor_tensor(hi_half, hi_half, rot[:, 1], ALU.add))
                    seen()
                assert steps == 16
                pool.wait_ge(lnv_ready, l + 1)
                root(lnr, lnr).then_inc(lnr_ready, 1)
                norm(l, 2)

        @block.tensor
        def _(pe):
            def products(out, lhs, rhs, start, stop, skip=False):
                (lh, ll), (rh, rl) = lhs, rhs
                nc.tensor.matmul(out, lh, rh, start=start, stop=False, skip_group_check=skip)
                nc.tensor.matmul(out, lh, rl, start=False, stop=False, skip_group_check=skip)
                return nc.tensor.matmul(out, ll, rh, start=False, stop=stop, skip_group_check=skip)

            def hT(k, t=None):
                s = slice(0, SEQ) if t is None else slice(t * P, (t + 1) * P)
                return hThi[:, k, s], hTlo[:, k, s]

            def gT(k, t):
                return gThi[:, k, t * P:(t + 1) * P], gTlo[:, k, t * P:(t + 1) * P]

            def wt(u0, n, k, row, cols):
                return view(whi, u0, n, k)[:, row, cols], view(wlo, u0, n, k)[:, row, cols]

            def norm(l, n, t):
                pe.wait_ge(h_ready, l * (3 * TT) + (n * TT + t + 2))
                for h in range(2):
                    if t:
                        pe.wait_ge(nlo, per_norm_half(l, n, 0, h))
                    for k in range(4):
                        o = t * D + (4 * h + k) * P
                        ins = nc.tensor.transpose(bank[:, 6 + h, k * P:(k + 1) * P], htok[:, o:o + P], ident[:, :])
                    ins.then_inc(ntr, 1)

            def ffn(l, f):
                n = 2 * f

                def gate_up(c, c0, t):
                    if not isinstance(c, int) or c > 0:
                        pe.wait_ge(gu_ready, per_ffn(l, f, c - 1, t))
                    for h in range(2):
                        if isinstance(c, int) and c == 0:
                            pe.wait_ge(nlo, per_norm_half(l, n, t, h))
                        if t == 0:
                            unit_waits(pe, l, unit_gu(f, c, h))
                        for k in range(4):
                            ins = products(bank[:, 4 + t, :], hT(4 * h + k, t),
                                           wt(unit_gu(f, c0, h), 2048, 4, k, slice(0, 2 * FC)),
                                           start=(h == 0 and k == 0), stop=(h == 1 and k == 3))
                        if t == 1:
                            ins.then_inc(unit_free, 1)
                        elif h == 1:
                            ins.then_inc(gu_done, 1)

                def turn(c, t):
                    pe.wait_ge(gu_ready, per_ffn(l, f, c, t))
                    if isinstance(c, int) and c == 0:
                        pe.wait_ge(nlo, per_norm_half(l, n, 1, 1))
                    else:
                        pe.wait_ge(glo, per_ffn(l, f, c - 1, t))
                    for k in range(2):
                        ins = nc.tensor.transpose(bank[:, 6 + t, k * P:(k + 1) * P], gu[:, t, k * P:(k + 1) * P],
                                                  ident[:, :])
                    ins.then_inc(gtr, 1)

                def down(c, c0, t, last=False):
                    pe.wait_ge(glo, per_ffn(l, f, c, t))
                    if t == 0:
                        unit_waits(pe, l, unit_down(f, c))
                    for k in range(2):
                        for m in range(2):
                            ins = products(bank[:, 2 * t + m, :], gT((c0 % 2) * 2 + k, t),
                                           wt(unit_down(f, c0), 2048, 2, k, slice(m * 512, (m + 1) * 512)),
                                           start=False, stop=last and k == 1, skip=True)
                    if t == 1:
                        ins.then_inc(unit_free, 1)
                    elif last:
                        ins.then_inc(acc_done, 1)

                def first():
                    norm(l, n, 0)
                    gate_up(0, 0, 0)
                    norm(l, n, 1)
                    for b in range(4):
                        nc.tensor.matmul(bank[:, b, :], zero[:, 0:P], zero[:, :], start=True, stop=False,
                                         skip_group_check=True)
                    gate_up(0, 0, 1)
                    turn(0, 0)

                def pair(c, c0):
                    gate_up(c, c0, 0)
                    turn(c - 1, 1)
                    gate_up(c, c0, 1)
                    down(c - 1, c0 - 1, 0)
                    turn(c, 0)
                    down(c - 1, c0 - 1, 1)

                def last():
                    pair(NCH - 2, NCH - 2)
                    pair(NCH - 1, NCH - 1)
                    turn(NCH - 1, 1)
                    down(NCH - 1, NCH - 1, 0, last=True)
                    down(NCH - 1, NCH - 1, 1, last=True)

                chunks(pe, f, first, pair, last)

            def conv_in(l, j, base, b0):
                for g in range(2):
                    u = UM + base + g
                    unit_waits(pe, l, u)
                    for ct in range(2):
                        for k in range(KD):
                            ins = products(bank[:, b0 + g, ct * SEQ:(ct + 1) * SEQ],
                                           wt(u, 2048, KD, k, slice(ct * P, (ct + 1) * P)), hT(k),
                                           start=(k == 0), stop=(k == KD - 1))
                    ins.then_inc(unit_free, 1)

            def head_turn(l, h):
                if h == 0:
                    pe.wait_ge(pool_step, (l + 1) * 16)
                else:
                    pe.wait_ge(qkt_ready, l * H + h)
                for j, tok in enumerate((qtok, ktok)):
                    for t in range(TT):
                        o = j * SEQ + t * P
                        ins = nc.tensor.transpose(bank[0:QK, 4, o:o + P], tok[:, t, h, :], ident[:, :])
                ins.then_inc(qkt_done, 1)

            def head_scores(l, h):
                pe.wait_ge(qkt_ready, l * H + h + 1)
                if h:
                    pe.wait_ge(max_ready, l * (2 * H) + 2 * h)
                q = qkT[0:QK, h % 2, :]
                nc.tensor.matmul(bank[:, 5, 0:P], q[:, 0:P], q[:, SEQ:SEQ + P], start=True, stop=True)
                nc.tensor.matmul(bank[:, 5, P:3 * P], q[:, P:2 * P], q[:, SEQ:2 * SEQ], start=True,
                                 stop=True).then_inc(s_done, 1)

            def head_probs(l, h):
                pe.wait_ge(exp_ready, l * H + h + 1)
                if h:
                    pe.wait_ge(pt_ready, l * H + h)
                nc.tensor.transpose(bank[:, 6, 0:P], prob[:, 0, 0:P], ident[:, :])
                nc.tensor.transpose(bank[:, 6, P:2 * P], prob[:, 1, 0:P], ident[:, :])
                nc.tensor.transpose(bank[:, 6, 2 * P:3 * P], prob[:, 1, P:2 * P], ident[:, :]).then_inc(pt_done, 1)

            def head_values(l, h):
                pe.wait_ge(pt_ready, l * H + h + 1)
                if h:
                    pe.wait_ge(o_ready, l * H + h)
                p = pT[:, h % 2, :]
                nc.tensor.matmul(bank[:, 7, 0:VD], p[:, 0:P], vtok[:, 0, h, :], start=True, stop=True)
                nc.tensor.matmul(bank[:, 7, VD:2 * VD], p[:, P:2 * P], vtok[:, 0, h, :], start=True, stop=False)
                nc.tensor.matmul(bank[:, 7, VD:2 * VD], p[:, 2 * P:3 * P], vtok[:, 1, h, :], start=False,
                                 stop=True).then_inc(pv_done, 1)

            def rows_out(l, u, units, lhs, t, b0, done):
                for i in range(units):
                    if t == 0:
                        unit_waits(pe, l, u + i)
                    for k in range(2):
                        for m in range(2):
                            ins = products(bank[:, b0 + m, :], lhs(2 * i + k, t),
                                           wt(u + i, 2048, 2, k, slice(m * 512, (m + 1) * 512)),
                                           start=(i == 0 and k == 0), stop=(i == units - 1 and k == 1))
                    if t == 1:
                        ins.then_inc(unit_free, 1)
                    elif i == units - 1:
                        ins.then_inc(done, 1)

            def mixer(l):
                for t in range(TT):
                    norm(l, 1, t)
                    for h in range(2):
                        u = UM + M_PR + h
                        if t == 0:
                            unit_waits(pe, l, u)
                        pe.wait_ge(nlo, per_norm_half(l, 1, t, h))
                        for k in range(4):
                            for m in range(2):
                                ins = products(bank[:, 2 * t + m, 0:PR // 2], hT(4 * h + k, t),
                                               wt(u, 4 * PR, 4, k, slice(m * PR // 2, (m + 1) * PR // 2)),
                                               start=(h == 0 and k == 0), stop=(h == 1 and k == 3))
                        if t == 1:
                            ins.then_inc(unit_free, 1)
                        elif h == 1:
                            ins.then_inc(pr_done, 1)
                conv_in(l, 0, M_C01, 4)
                for j in range(2):
                    pe.wait_ge(pr_norm, l + 1)
                    for k in range(2):
                        for t in range(TT):
                            o = (k * TT + t) * P
                            ins = nc.tensor.transpose(bank[:, 6 + j, o:o + P],
                                                      pr[:, t, (2 * j + k) * P:(2 * j + k + 1) * P], ident[:, :])
                    ins.then_inc(lat_tr, 1)
                for t in range(TT):
                    if t == 0:
                        unit_waits(pe, l, UM + M_UQ)
                        pe.wait_ge(lat_lo, l * 4 + 2)
                    for k in range(2):
                        for m in range(2):
                            ins = products(bank[:, 2 * t + m, 0:4 * QK], gT(k, t),
                                           wt(UM + M_UQ, 2 * H * QK, 2, k, slice(m * 4 * QK, (m + 1) * 4 * QK)),
                                           start=(k == 0), stop=(k == 1))
                    ins.then_inc(unit_free if t else q_done, 1)
                for t in range(TT):
                    if t == 0:
                        unit_waits(pe, l, UM + M_UKV)
                        pe.wait_ge(lat_lo, l * 4 + 4)
                        pe.wait_ge(cu_ready, l * 2 + 1)
                    for k in range(2):
                        for m in range(2):
                            ins = products(bank[:, 4 + 2 * t + m, :], gT(2 + k, t),
                                           wt(UM + M_UKV, 2048, 2, k, slice(m * 512, (m + 1) * 512)),
                                           start=(k == 0), stop=(k == 1))
                    ins.then_inc(unit_free if t else kv_done, 1)
                pe.wait_ge(q_ready, l * 4 + 2)
                conv_in(l, 1, M_C23, 0)
                for u8 in range(8):
                    g, kh = u8 // 2, u8 % 2
                    b0 = 2 if g % 2 == 0 else 0
                    u = UM + M_G + u8
                    if u8 == 0:
                        pe.wait_ge(kv_ready, l * 8 + 8)
                    if u8 >= 1:
                        head_turn(l, u8 - 1)
                    for t in range(TT):
                        if t == 0:
                            unit_waits(pe, l, u)
                        if kh == 0:
                            if g == 0:
                                pe.wait_ge(q_ready, l * 4 + 4)
                            elif g == 1:
                                pe.wait_ge(cu_ready, l * 2 + 2)
                            else:
                                pe.wait_ge(gate_sum, l * 8 + ((g - 2) * 2 + t + 1))
                        for k in range(4):
                            ins = products(bank[:, b0 + t, :], hT(4 * kh + k, t), wt(u, 2048, 4, k, slice(0, 512)),
                                           start=(kh == 0 and k == 0), stop=(kh == 1 and k == 3))
                        if t == 1:
                            ins.then_inc(unit_free, 1)
                        elif kh == 1:
                            ins.then_inc(gate_done, 1)
                        if t == 0 and u8 >= 1:
                            if u8 >= 2:
                                head_probs(l, u8 - 2)
                            head_scores(l, u8 - 1)
                    if u8 >= 2:
                        head_values(l, u8 - 2)
                head_turn(l, H - 1)
                head_probs(l, H - 2)
                head_scores(l, H - 1)
                head_values(l, H - 2)
                head_probs(l, H - 1)
                head_values(l, H - 1)
                for t in range(TT):
                    if t == 0:
                        pe.wait_ge(o_ready, (l + 1) * H)
                    for k in range(4):
                        ins = nc.tensor.transpose(bank[:, 4 + t, k * P:(k + 1) * P], otok[:, t, k * P:(k + 1) * P],
                                                  ident[:, :])
                    ins.then_inc(ot_done, 1)
                for t in range(TT):
                    pe.wait_ge(ot_lo, l * 2 + t + 1)
                    pe.wait_ge(gate_sum, l * 8 + (6 if t == 0 else 8))
                    rows_out(l, UM + M_MLA, 2, hT, t, 2 - 2 * t, mla_done)
                pe.wait_ge(tap, (l + 1) * N_TAP)
                for ct in range(CT):
                    ins = nc.tensor.matmul(bank[:, 6, 0:SEQ], mean_of[:, :], cacc[:, ct, :], start=(ct == 0),
                                           stop=(ct == CT - 1))
                ins.then_inc(mean_done, 1)
                pe.wait_ge(csq_ready, l + 1)
                for ct in range(CT):
                    ins = nc.tensor.matmul(bank[:, 6, SEQ:2 * SEQ], mean_of[:, :], csq[:, ct, :], start=(ct == 0),
                                           stop=(ct == CT - 1))
                ins.then_inc(var_done, 1)
                pe.wait_ge(c_lo, l + 1)
                for t in range(TT):
                    rows_out(l, UM + M_CO, 2, gT, t, 4 + 2 * t, co_done)
                for t in range(TT):
                    for h in range(2):
                        pe.wait_ge(y_ready, l * 4 + t * 2 + h + 1)
                        for k in range(4):
                            o = (4 * h + k) * P
                            ins = nc.tensor.transpose(bank[:, 2 * t + h, k * P:(k + 1) * P], gates[:, t, o:o + P],
                                                      ident[:, :])
                        ins.then_inc(yt_done, 1)
                    pe.wait_ge(yt_lo, l * 4 + t * 2 + 2)
                    rows_out(l, UM + M_WO, 4, hT, t, 4 - 2 * t, acc_done)

            pe.sem_inc(unit_free, RING)
            pe.wait_ge(const_ready, 4)
            pe.wait_ge(dve_const, 1)
            with pe.Fori(0, DEPTH) as l:
                ffn(l, 0)
                mixer(l)
                ffn(l, 1)


        @block.scalar
        def _(act):
            def split(l, u0, turns=0):
                n = (l * (U_LAYER // RAW) + turns + (u0 // RAW + 1)) * 32
                act.wait_ge(raw_landed[slot(u0, RAW)], n)
                act.wait_ge(unit_free, l * U_LAYER + turns * RAW + (u0 + 1))
                nc.scalar.activation(whi[:, slot(u0, RING), 0:USED[u0]], raw[:, slot(u0, RAW), 0:USED[u0]],
                                     ACT.Copy).then_inc(whi_ready, 1)

            def norm_squares(l, n, t):
                act.wait_ge(x_new, l * 6 + (n * TT + t + 1))
                nc.scalar.activation(htok[:, t * D:(t + 1) * D], x[:, t, :], ACT.Square,
                                     accum_out=ss[:, t:t + 1]).then_inc(sq_ready, 1)

            def norm_round(l, n, t):
                for h in range(2):
                    act.wait_ge(ntr, per_norm_half(l, n, t, h))
                    nc.scalar.activation(hThi[:, 4 * h:4 * h + 4, t * P:(t + 1) * P],
                                         bank[:, 6 + h, :].rearrange("p (k n) -> p k n", k=4),
                                         ACT.Copy).then_inc(nhi, 1)

            def ffn(l, f):
                def silu(c, t):
                    if t == 0:
                        act.wait_ge(gu_done, l * (2 * NCH) + c + (NCH * f + 1))
                    else:
                        unit_released(act, l, unit_gu(f, c, 1))
                    nc.scalar.activation(sgate[:, t, :], bank[:, 4 + t, 0:FC], ACT.Silu).then_inc(silu_ready, 1)

                def round_gu(c, c0, t):
                    act.wait_ge(gtr, per_ffn(l, f, c, t))
                    if not (isinstance(c, int) and c == 0):
                        unit_released(act, l, c * 3 + (UB[f] - 2))
                    nc.scalar.activation(gThi[:, (c0 % 2) * 2:(c0 % 2) * 2 + 2, t * P:(t + 1) * P],
                                         bank[:, 6 + t, 0:2 * P].rearrange("p (k n) -> p k n", k=2),
                                         ACT.Copy).then_inc(ghi, 1)

                def first():
                    silu(0, 0)
                    silu(0, 1)
                    round_gu(0, 0, 0)

                def pair(c, c0, i=0):
                    u = UB[f] + 2 + 3 * c0
                    split(l, u, i)
                    silu(c, 0)
                    round_gu(c - 1, c0 - 1, 1)
                    split(l, u + 1, i)
                    silu(c, 1)
                    round_gu(c, c0, 0)
                    split(l, u + 2, i)

                first()
                with act.Fori(0, (NCH - 3) // 2) as i:
                    pair(i * 2 + 1, 1, i * 2)
                    pair(i * 2 + 2, 2, i * 2)
                pair(NCH - 2, NCH - 2)
                c = NCH - 1
                if f == 0:
                    split(l, UB[f] + 2 + 3 * c)
                else:
                    split(l, UB[f] + U_FFN - 1)
                silu(c, 0)
                round_gu(c - 1, c - 1, 1)
                if f == 0:
                    split(l, UB[f] + 3 + 3 * c)
                silu(c, 1)
                round_gu(c, c, 0)
                if f == 0:
                    split(l, UB[f] + 4 + 3 * c)
                round_gu(c, c, 1)

            def mixer(l):
                s = iter(range(UM + LEAD, UM + U_MIX + LEAD))

                def one():
                    split(l, next(s))

                def load_bias(g):
                    act.dma_start(bias[:, :], a["gate_bias"][l, g // 2:g // 2 + 1, (g % 2) * C:(g % 2 + 1) * C]
                                  .to_broadcast([P, C])).then_inc(bias_landed, 16)

                load_bias(0)
                one()
                for t in range(TT):
                    if t == 0:
                        act.wait_ge(pr_done, l + 1)
                    else:
                        unit_released(act, l, UM + M_PR + 1)
                    nc.scalar.activation(pr[:, t, :].rearrange("p (m n) -> p m n", m=2),
                                         bank[:, 2 * t:2 * t + 2, 0:PR // 2], ACT.Copy).then_inc(pr_ready, 1)
                    act.wait_ge(pr_ready, l * 2 + t + 1)
                    for j in range(2):
                        nc.scalar.activation(junk[:, t, j * QL:(j + 1) * QL], pr[:, t, j * QL:(j + 1) * QL], ACT.Square,
                                             accum_out=ss4[:, 2 * t + j:2 * t + j + 1]).then_inc(pr_sq, 1)
                one()
                act.wait_ge(vec_landed, (l + 1) * 48)
                for j in range(2):
                    act.wait_ge(lat_tr, l * 2 + j + 1)
                    for k in range(2):
                        nc.scalar.activation(gThi[:, 2 * j + k, :], bank[:, 6 + j, k * SEQ:(k + 1) * SEQ], ACT.Copy,
                                             scale=vec[:, V_CQ + 2 * j + k:V_CQ + 2 * j + k + 1]).then_inc(lat_hi, 1)
                unit_released(act, l, UM + M_C01 + 1)
                nc.scalar.activation(cacc[:, 0:2, :].rearrange("p c n -> p (c n)"), bank[:, 5, :], ACT.Tanh,
                                     scale=0.5).then_inc(tanh_ready, 1)
                one()
                one()
                for t in range(TT):
                    if t == 0:
                        act.wait_ge(q_done, l + 1)
                    else:
                        unit_released(act, l, UM + M_UQ)
                    for m in range(2):
                        nc.scalar.activation(qtok[:, t, 4 * m:4 * m + 4, :].rearrange("p h d -> p (h d)"),
                                             bank[:, 2 * t + m, 0:4 * QK], ACT.Copy).then_inc(q_ready, 1)
                act.wait_ge(q_ready, (l + 1) * 4)
                nc.scalar.activation(junk, qtok.rearrange("p t h d -> p t (h d)"),
                                     ACT.Square).then_inc(qk_sq, 1)
                one()
                for t in range(TT):
                    if t == 0:
                        act.wait_ge(kv_done, l + 1)
                    else:
                        unit_released(act, l, UM + M_UKV)
                    for m in range(2):
                        kv = bank[:, 4 + 2 * t + m, :].rearrange("p (h d) -> p h d", h=4)
                        nc.scalar.activation(ktok[:, t, 4 * m:4 * m + 4, 0:NOPE], kv[:, :, 0:NOPE],
                                             ACT.Copy).then_inc(kv_ready, 1)
                        nc.scalar.activation(vtok[:, t, 4 * m:4 * m + 4, :], kv[:, :, NOPE:NOPE + VD],
                                             ACT.Copy).then_inc(kv_ready, 1)
                    nc.scalar.activation(ktok[:, t, :, NOPE:QK],
                                         pr[:, t:t + 1, QL + KVL:PR].to_broadcast([P, H, ROPE]),
                                         ACT.Copy).then_inc(kr_ready, 1)
                act.wait_ge(kv_ready, (l + 1) * 8)
                act.wait_ge(kr_ready, (l + 1) * 2)
                act.wait_ge(qk_sum, l * 2 + 1)
                nc.scalar.activation(junk, ktok[:, :, :, :].rearrange("p t h d -> p t (h d)"),
                                     ACT.Square).then_inc(qk_sq, 1)
                one()
                unit_released(act, l, UM + M_C23 + 1)
                nc.scalar.activation(cacc[:, 2:4, :].rearrange("p c n -> p (c n)"), bank[:, 1, :], ACT.Tanh,
                                     scale=0.5).then_inc(tanh_ready, 1)
                one()
                one()

                def head_copy(h):
                    act.wait_ge(qkt_done, l * H + h + 1)
                    nc.scalar.activation(qkT[0:QK, h % 2, :], bank[0:QK, 4, :], ACT.Copy).then_inc(qkt_ready, 1)

                def head_exp(h):
                    act.wait_ge(nmx_ready, l * H + h + 1)
                    nc.scalar.activation(prob[:, 0, 0:P], prob[:, 0, 0:P], ACT.Exp, bias=nmx[:, 0:1], scale=SCALE,
                                         accum_out=psum_h[:, 0:1])
                    nc.scalar.activation(prob[:, 1, :], prob[:, 1, :], ACT.Exp, bias=nmx[:, 1:2], scale=SCALE,
                                         accum_out=psum_h[:, 1:2]).then_inc(exp_ready, 1)

                def head_probs(h):
                    act.wait_ge(pt_done, l * H + h + 1)
                    nc.scalar.activation(pT[:, h % 2, :], bank[:, 6, 0:3 * P], ACT.Copy).then_inc(pt_ready, 1)

                for u8 in range(8):
                    if u8 >= 1:
                        head_copy(u8 - 1)
                    one()
                    if u8 >= 2:
                        head_probs(u8 - 2)
                    if u8 >= 1:
                        head_exp(u8 - 1)
                    if u8 % 2:
                        g = u8 // 2
                        for t in range(TT):
                            act.wait_ge(gate_sum, l * 8 + (g * 2 + t + 1))
                            o = gates[:, t, g * C:(g + 1) * C]
                            nc.scalar.activation(o, o, ACT.Tanh, scale=0.5).then_inc(gate_ready, 1)
                        if g < 3:
                            load_bias(g + 1)
                head_copy(H - 1)
                head_probs(H - 2)
                head_exp(H - 1)
                head_probs(H - 1)
                one()
                for t in range(TT):
                    act.wait_ge(ot_done, l * 2 + t + 1)
                    nc.scalar.activation(hThi[:, 0:4, t * P:(t + 1) * P],
                                         bank[:, 4 + t, :].rearrange("p (k n) -> p k n", k=4),
                                         ACT.Copy).then_inc(ot_hi, 1)
                act.dma_start(gain[:, :], norms[2][bass.ds(l, 1), :].to_broadcast([P, D])).then_inc(gain_landed, 16)
                one()
                act.wait_ge(xc_ready, l + 1)
                nc.scalar.activation(csq, cacc[:, :, :], ACT.Square).then_inc(csq_ready, 1)
                one()
                act.wait_ge(ln_ready, l + 1)
                for ct in range(CT):
                    nc.scalar.activation(cacc[:, ct, :], cacc[:, ct, :], ACT.Silu,
                                         scale=vec[:, V_LG + ct:V_LG + ct + 1],
                                         bias=vec[:, V_LB + ct:V_LB + ct + 1]).then_inc(act_silu, 1)
                act.wait_ge(act_silu, (l + 1) * CT)
                nc.scalar.activation(gThi[:, :, :], cacc[:, :, :], ACT.Copy).then_inc(c_hi, 1)
                for t in range(TT):
                    for h in range(2):
                        act.wait_ge(yt_done, l * 4 + t * 2 + h + 1)
                        nc.scalar.activation(hThi[:, 4 * h:4 * h + 4, t * P:(t + 1) * P],
                                             bank[:, 2 * t + h, :].rearrange("p (k n) -> p k n", k=4),
                                             ACT.Copy).then_inc(yt_hi, 1)
                    if t == 0:
                        one()
                        one()
                assert next(s) == UB[1] + 2

            act.wait_ge(rope_step, N_ROPE)
            nc.scalar.activation(cossin[:, 1, :, :], ang[:, 0, :, :], ACT.Sin).then_inc(trig_ready, 1)
            nc.scalar.activation(cossin[:, 0, :, :], ang[:, 1, :, :], ACT.Sin).then_inc(trig_ready, 1)
            with act.Fori(0, DEPTH) as l:
                for u in range(2):
                    split(l, u)
                for n, (stage, lead) in enumerate(((lambda: ffn(l, 0), 0), (lambda: mixer(l), UM),
                                                   (lambda: ffn(l, 1), UB[1]))):
                    for t in range(TT):
                        norm_squares(l, n, t)
                        norm_round(l, n, t)
                    for u in range(lead + 2, lead + LEAD):
                        split(l, u)
                    stage()

        @block.vector
        def _(dve):
            def split(l, u0, turns=0):
                dve.wait_ge(whi_ready, l * U_LAYER + turns * RAW + (u0 + 1))
                n = USED[u0]
                nc.vector.tensor_tensor(wlo[:, slot(u0, RING), 0:n], raw[:, slot(u0, RAW), 0:n],
                                        whi[:, slot(u0, RING), 0:n].bitcast(F32),
                                        ALU.subtract).then_inc(wlo_ready, 1)

            def rest(out, in_, hi):
                return nc.vector.tensor_tensor(out, in_, hi.bitcast(F32), ALU.subtract)

            def norm_scale(l, n, t):
                dve.wait_ge(sq_ready, per_norm(l, n, t))
                nc.vector.tensor_scalar(ms[:, t:t + 1], ss[:, t:t + 1], 1.0 / D, EPS, ALU.mult,
                                        ALU.add).then_inc(ms_ready, 1)

            def norm_apply(l, n, t):
                dve.wait_ge(rs_ready, per_norm(l, n, t))
                if t == 0:
                    dve.wait_ge(gain_landed, l * 48 + 16 * (n + 1))
                nc.vector.scalar_tensor_tensor(out=htok[:, t * D:(t + 1) * D], in0=x[:, t, :],
                                               scalar=rs[:, t:t + 1], in1=gain[:, :], op0=ALU.mult,
                                               op1=ALU.mult).then_inc(h_ready, 1)

            def norm_rest(l, n, t):
                for h in range(2):
                    dve.wait_ge(nhi, per_norm_half(l, n, t, h))
                    rest(hTlo[:, 4 * h:4 * h + 4, t * P:(t + 1) * P],
                         bank[:, 6 + h, :].rearrange("p (k n) -> p k n", k=4),
                         hThi[:, 4 * h:4 * h + 4, t * P:(t + 1) * P]).then_inc(nlo, 1)

            def residual(l, stage, t, b0, u_last):
                if t == 0:
                    dve.wait_ge(acc_done, l * 3 + stage + 1)
                else:
                    unit_released(dve, l, u_last)
                nc.vector.scalar_tensor_tensor(out=x[:, t, :], in0=bank[:, b0:b0 + 2, :].rearrange("p b n -> p (b n)"),
                                               scalar=0.5, in1=x[:, t, :], op0=ALU.mult,
                                               op1=ALU.add).then_inc(x_new, 1)

            def ffn(l, f):
                def mul(c, t):
                    dve.wait_ge(silu_ready, per_ffn(l, f, c, t))
                    if not (isinstance(c, int) and c == 0):
                        dve.wait_ge(gtr, per_ffn(l, f, c - 1, t))
                    nc.vector.tensor_tensor(gu[:, t, :], sgate[:, t, :], bank[:, 4 + t, FC:2 * FC],
                                            ALU.mult).then_inc(gu_ready, 1)

                def rest_gu(c, c0, t):
                    dve.wait_ge(ghi, per_ffn(l, f, c, t))
                    o = gThi[:, (c0 % 2) * 2:(c0 % 2) * 2 + 2, t * P:(t + 1) * P]
                    rest(gTlo[:, (c0 % 2) * 2:(c0 % 2) * 2 + 2, t * P:(t + 1) * P],
                         bank[:, 6 + t, 0:2 * P].rearrange("p (k n) -> p k n", k=2), o).then_inc(glo, 1)

                def pair(c, c0, i=0):
                    u = UB[f] + 2 + 3 * c0
                    split(l, u, i)
                    mul(c, 0)
                    rest_gu(c - 1, c0 - 1, 1)
                    split(l, u + 1, i)
                    mul(c, 1)
                    rest_gu(c, c0, 0)
                    split(l, u + 2, i)

                mul(0, 0)
                mul(0, 1)
                rest_gu(0, 0, 0)
                with dve.Fori(0, (NCH - 3) // 2) as i:
                    pair(i * 2 + 1, 1, i * 2)
                    pair(i * 2 + 2, 2, i * 2)
                pair(NCH - 2, NCH - 2)
                c = NCH - 1
                if f == 0:
                    split(l, UB[f] + 2 + 3 * c)
                else:
                    split(l, UB[f] + U_FFN - 1)
                mul(c, 0)
                rest_gu(c - 1, c - 1, 1)
                if f == 0:
                    split(l, UB[f] + 3 + 3 * c)
                mul(c, 1)
                rest_gu(c, c, 0)
                if f == 0:
                    split(l, UB[f] + 4 + 3 * c)
                rest_gu(c, c, 1)

            def mixer(l):
                s = iter(range(UM + LEAD, UM + U_MIX + LEAD))
                done = [0]
                seen = {}

                def one():
                    split(l, next(s))

                def conv(ct, k):
                    if ct in seen:
                        dve.wait_ge(tap, l * N_TAP + seen[ct])
                    o = cacc[:, ct, :]
                    if k == W:
                        ins = nc.vector.tensor_scalar(o, o, 0.5, vec[:, V_CB + ct:V_CB + ct + 1], ALU.mult, ALU.add)
                    else:
                        i = cu[:, ct, k:k + SEQ]
                        w = vec[:, V_W + ct * W + k:V_W + ct * W + k + 1]
                        if k == 0:
                            ins = nc.vector.tensor_scalar(o, i, w, None, ALU.mult)
                        else:
                            ins = nc.vector.scalar_tensor_tensor(out=o, in0=i, scalar=w, in1=o, op0=ALU.mult,
                                                                 op1=ALU.add)
                    ins.then_inc(tap, 1)
                    done[0] += 1
                    seen[ct] = done[0]

                work = [iter([(ct, k) for k in range(W + 1) for ct in (2 * j, 2 * j + 1)]) for j in range(2)]

                def taps(n):
                    for _ in range(n):
                        for w in work[:(2 if len(ready) > 1 else 1)]:
                            nxt = next(w, None)
                            if nxt:
                                conv(*nxt)
                                break

                ready = []

                def conv_gate(j, b0):
                    dve.wait_ge(tanh_ready, l * 2 + j + 1)
                    nc.vector.scalar_tensor_tensor(out=cu[:, 2 * j:2 * j + 2, W - 1:W - 1 + SEQ],
                                                   in0=cacc[:, 2 * j:2 * j + 2, :], scalar=1.0,
                                                   in1=bank[:, b0, :].rearrange("p (c n) -> p c n", c=2),
                                                   op0=ALU.add, op1=ALU.mult).then_inc(cu_ready, 1)
                    dve.wait_ge(cu_ready, l * 2 + j + 1)
                    ready.append(j)

                one()
                dve.wait_ge(pr_sq, (l + 1) * 4)
                nc.vector.tensor_scalar(ss4, ss4, 1.0 / QL, EPS, ALU.mult, ALU.add).then_inc(pr_ms, 1)
                one()
                dve.wait_ge(pr_rs, l + 1)
                lat = pr[:, :, 0:QL + KVL].rearrange("p t (j n) -> p t j n", j=2)
                nc.vector.tensor_tensor(lat, lat, rs4.rearrange("p (t j) -> p t j", t=2).unsqueeze(3)
                                        .to_broadcast([P, TT, 2, QL]), ALU.mult).then_inc(pr_norm, 1)
                dve.wait_ge(vec_landed, (l + 1) * 48)
                for j in range(2):
                    dve.wait_ge(lat_hi, l * 4 + 2 * j + 2)
                    for k in range(2):
                        nc.vector.scalar_tensor_tensor(out=gTlo[:, 2 * j + k, :],
                                                       in0=bank[:, 6 + j, k * SEQ:(k + 1) * SEQ],
                                                       scalar=vec[:, V_CQ + 2 * j + k:V_CQ + 2 * j + k + 1],
                                                       in1=gThi[:, 2 * j + k, :].bitcast(F32), op0=ALU.mult,
                                                       op1=ALU.subtract).then_inc(lat_lo, 1)
                conv_gate(0, 4)
                one()
                one()
                taps(8)
                one()
                for j, tok in enumerate((qtok, ktok[:, :, :, :])):
                    dve.wait_ge(qk_sq, l * 2 + j + 1)
                    sums = ssqk[:, 16 * j:16 * j + 16]
                    nc.vector.tensor_reduce(sums, junk.rearrange("p t (h d) -> p t h d", h=H), AX.X,
                                            ALU.add).then_inc(qk_sum, 1)
                    dve.wait_ge(qk_sum, l * 2 + j + 1)
                    nc.vector.tensor_scalar(sums, sums, 1.0 / QK, EPS, ALU.mult, ALU.add).then_inc(qk_ms, 1)
                    taps(3)
                    dve.wait_ge(qk_rs, l * 2 + j + 1)
                    r = rsqk[:, 16 * j:16 * j + 16].rearrange("p (t h) -> p t h", t=TT).unsqueeze(3)
                    nc.vector.tensor_tensor(tok, tok, r.to_broadcast([P, TT, H, QK]), ALU.mult).then_inc(qk_norm, 1)
                    one()
                conv_gate(1, 0)
                taps(6)
                one()

                def head_max(h):
                    dve.wait_ge(s_done, l * H + h + 1)
                    if h:
                        dve.wait_ge(pt_done, l * H + h)
                    else:
                        dve.wait_ge(pool_step, (l + 1) * 16)
                    nc.vector.memset(small[:, 94:95], 0.0)
                    nc.vector.tensor_tensor_reduce(out=prob[:, 0, 0:P], in0=bank[:, 5, 0:P], in1=mask[:, P:2 * P],
                                                   scale=1.0, scalar=-3e38, op0=ALU.add, op1=ALU.max,
                                                   accum_out=mx[:, 0:1]).then_inc(max_ready, 1)
                    nc.vector.tensor_tensor_reduce(out=prob[:, 1, :], in0=bank[:, 5, P:3 * P], in1=mask[:, :],
                                                   scale=1.0, scalar=-3e38, op0=ALU.add, op1=ALU.max,
                                                   accum_out=mx[:, 1:2]).then_inc(max_ready, 1)
                    dve.wait_ge(max_ready, l * (2 * H) + 2 * h + 2)
                    nc.vector.tensor_scalar(nmx, mx, -SCALE, None, ALU.mult).then_inc(nmx_ready, 1)

                def head_sum(h):
                    dve.wait_ge(exp_ready, l * H + h + 1)
                    nc.vector.reciprocal(rsum[h % 2], psum_h).then_inc(rsum_ready, 1)

                def head_out(h):
                    dve.wait_ge(pv_done, l * H + h + 1)
                    dve.wait_ge(rsum_ready, l * H + h + 1)
                    nc.vector.tensor_tensor(otok[:, :, h * VD:(h + 1) * VD], bank[:, 7, 0:2 * VD].rearrange("p (t d) -> p t d", t=TT),
                                            rsum[h % 2].unsqueeze(2).to_broadcast([P, TT, VD]),
                                            ALU.mult).then_inc(o_ready, 1)

                def gate_bias(g):
                    for t in range(TT):
                        if t == 0:
                            dve.wait_ge(gate_done, l * 4 + g + 1)
                            dve.wait_ge(bias_landed, l * 64 + 16 * (g + 1))
                        else:
                            unit_released(dve, l, UM + M_G + 2 * g + 1)
                        nc.vector.tensor_tensor(gates[:, t, g * C:(g + 1) * C], bank[:, (2 if g % 2 == 0 else 0) + t, :],
                                                bias[:, :], ALU.add).then_inc(gate_sum, 1)

                for u8 in range(8):
                    one()
                    taps(7)
                    if u8 >= 1:
                        head_max(u8 - 1)
                    taps(6)
                    if u8 >= 2:
                        head_out(u8 - 2)
                    if u8 >= 1:
                        head_sum(u8 - 1)
                    if u8 % 2:
                        gate_bias(u8 // 2)
                head_max(H - 1)
                head_out(H - 2)
                head_sum(H - 1)
                one()
                head_out(H - 1)
                for t in range(TT):
                    dve.wait_ge(ot_hi, l * 2 + t + 1)
                    rest(hTlo[:, 0:4, t * P:(t + 1) * P], bank[:, 4 + t, :].rearrange("p (k n) -> p k n", k=4),
                         hThi[:, 0:4, t * P:(t + 1) * P]).then_inc(ot_lo, 1)
                taps(200)
                one()
                assert done[0] == N_TAP

                def gated(t, half, b0, ready_sem):
                    o = gates[:, t, half * D:(half + 1) * D]
                    nc.vector.scalar_tensor_tensor(out=o, in0=o, scalar=1.0,
                                                   in1=bank[:, b0:b0 + 2, :].rearrange("p b n -> p (b n)"),
                                                   op0=ALU.add, op1=ALU.mult).then_inc(ready_sem, 1)

                dve.wait_ge(gate_ready, (l + 1) * 8)
                dve.wait_ge(mla_done, l + 1)
                gated(0, 1, 2, ym_ready)
                dve.wait_ge(mean_done, l + 1)
                nc.vector.tensor_tensor(cacc[:, :, :], cacc[:, :, :],
                                        bank[:, 6:7, 0:SEQ].to_broadcast([P, CT, SEQ]),
                                        ALU.subtract).then_inc(xc_ready, 1)
                unit_released(dve, l, UM + M_MLA + 1)
                gated(1, 1, 0, ym_ready)
                dve.wait_ge(var_done, l + 1)
                nc.vector.tensor_scalar(lnr, bank[:, 6, SEQ:2 * SEQ], EPS, None, ALU.add).then_inc(lnv_ready, 1)
                one()
                dve.wait_ge(lnr_ready, l + 1)
                dve.wait_ge(xc_ready, l + 1)
                nc.vector.tensor_tensor(cacc[:, :, :], cacc[:, :, :],
                                        lnr.unsqueeze(1).to_broadcast([P, CT, SEQ]),
                                        ALU.mult).then_inc(ln_ready, 1)
                dve.wait_ge(c_hi, l + 1)
                rest(gTlo[:, :, :], cacc[:, :, :], gThi[:, :, :]).then_inc(c_lo, 1)
                nc.vector.memset(small[:, 90:91], 0.0).then_inc(vec_used, 1)
                for t in range(TT):
                    if t == 0:
                        dve.wait_ge(co_done, l + 1)
                    else:
                        unit_released(dve, l, UM + M_CO + 1)
                    gated(t, 0, 4 + 2 * t, yc_ready)
                    dve.wait_ge(yc_ready, l * 2 + t + 1)
                    dve.wait_ge(ym_ready, l * 2 + 2)
                    for h in range(2):
                        o = gates[:, t, h * C:(h + 1) * C]
                        nc.vector.tensor_tensor(o, o, gates[:, t, D + h * C:D + (h + 1) * C],
                                                ALU.add).then_inc(y_ready, 1)
                    for h in range(2):
                        dve.wait_ge(yt_hi, l * 4 + t * 2 + h + 1)
                        rest(hTlo[:, 4 * h:4 * h + 4, t * P:(t + 1) * P],
                             bank[:, 2 * t + h, :].rearrange("p (k n) -> p k n", k=4),
                             hThi[:, 4 * h:4 * h + 4, t * P:(t + 1) * P]).then_inc(yt_lo, 1)
                    if t == 0:
                        one()
                        one()
                assert next(s) == UB[1] + 2

            nc.vector.memset(zero[:, :], 0.0).then_inc(dve_const, 1)
            nc.vector.memset(mask[:, :], 0.0).then_inc(dve_const, 1)
            nc.vector.memset(cu[:, :, 0:W - 1], 0.0)
            dve.wait_ge(dve_const, 2)
            nc.vector.memset(mask[0:CHUNK, P + CHUNK:2 * P], MASKED)
            dve.sem_inc(wlo_ready, RAW)
            dve.sem_inc(vec_used, 1)
            dve.sem_inc(h_ready, 1)
            dve.wait_ge(x_landed, 16 * TT)
            dve.sem_inc(x_new, TT)

            rstep = [0]

            def r(ins):
                rstep[0] += 1
                ins.then_inc(rope_step, 1)
                dve.wait_ge(rope_step, rstep[0])

            A, B2, KH, K2 = (ang[:, i, :, :] for i in range(4))
            dve.wait_ge(small_landed, 16 * TT)
            freq = [float(np.float32(10000.0) ** np.float32(-i / ROPE)) for i in range(0, ROPE, 2)]
            r(nc.vector.tensor_copy(small[:, 91:93], posi[:, :]))
            for i in range(HALF):
                ins = nc.vector.tensor_scalar(ang[:, 0, :, i], small[:, 91:93], freq[i], None, ALU.mult)
            r(ins)
            two_pi = 2 * np.pi
            big = 65536.0
            magic = 1.5 * 2 ** 23

            def turns(out, period):
                r(nc.vector.tensor_scalar(out, A, 1.0 / period, magic, ALU.mult, ALU.add))
                r(nc.vector.tensor_scalar(out, out, magic, None, ALU.subtract))

            def less(k, part):
                r(nc.vector.scalar_tensor_tensor(out=A, in0=k, scalar=-part, in1=A, op0=ALU.mult, op1=ALU.add))

            parts_big = two_pi_parts(two_pi * big, (2.0 ** 11, 2.0 ** 3, 2.0 ** -5))
            parts = two_pi_parts(two_pi, (2.0 ** -5, 2.0 ** -13, 2.0 ** -21))
            turns(KH, two_pi * big)
            for part in parts_big[:3]:
                less(KH, part)
            turns(K2, two_pi)
            for part in parts:
                less(K2, part)
            less(KH, parts_big[3])
            turns(K2, two_pi)
            for part in parts:
                less(K2, part)
            lim = float(np.nextafter(np.float32(np.pi), np.float32(0)))
            r(nc.vector.tensor_scalar(A, A, lim, -lim, ALU.min, ALU.max))
            r(nc.vector.tensor_scalar(KH, A, -1.0, None, ALU.mult))
            r(nc.vector.tensor_tensor(KH, KH, A, ALU.max))
            r(nc.vector.tensor_scalar(B2, KH, -1.0, float(np.float32(np.pi / 2)), ALU.mult, ALU.add))
            assert rstep[0] == N_ROPE

            with dve.Fori(0, DEPTH) as l:
                def norm(n, t):
                    norm_scale(l, n, t)
                    norm_apply(l, n, t)
                    norm_rest(l, n, t)

                for u in range(2):
                    split(l, u)
                for t in range(TT):
                    norm(0, t)
                for u in range(2, LEAD):
                    split(l, u)
                ffn(l, 0)
                for t in range(TT):
                    residual(l, 0, t, 2 * t, UB[0] + U_FFN - 1)
                    norm(1, t)
                for u in range(UM + 2, UM + LEAD):
                    split(l, u)
                mixer(l)
                for t in range(TT):
                    residual(l, 1, t, 4 - 2 * t, UM + U_MIX - 1)
                    norm(2, t)
                for u in range(UB[1] + 2, UB[1] + LEAD):
                    split(l, u)
                ffn(l, 1)
                for t in range(TT):
                    residual(l, 2, t, 2 * t, UB[1] + U_FFN - 1)


_BIG = ["x", "positions", "ffn1_norm", "ffn1_w_gate", "ffn1_w_up", "ffn1_w_down", "mix_norm", "w_in", "gate_bias",
        "w_conv_out", "w_uq", "w_ukv", "q_norm", "k_norm", "w_mla_out", "w_out", "ffn2_norm", "ffn2_w_gate",
        "ffn2_w_up", "ffn2_w_down"]


def kernel(**inputs):
    import concourse.bacc as bacc
    from concourse.bass_utils import run_bass_kernel_spmd

    def tiles(v):
        return v.reshape(DEPTH, -1, P).transpose(0, 2, 1)

    arrays = {n: np.ascontiguousarray(inputs[n]) for n in _BIG}
    taps = np.asarray(inputs["conv_w"]).reshape(DEPTH, W, CT, P).transpose(0, 3, 2, 1).reshape(DEPTH, P, CT * W)
    arrays["vec"] = np.ascontiguousarray(np.concatenate(
        [taps] + [tiles(np.asarray(inputs[n])) for n in ("conv_b", "conv_ln_g", "conv_ln_b", "cq_norm", "ckv_norm")],
        axis=2))
    nc = bacc.Bacc("TRN2", target_bir_lowering=False, num_devices=1, dynamic_dma_scratch_size=1024)
    args = {n: nc.dram_tensor(f"in_{n}", v.shape, mybir.dt.from_np(v.dtype), kind="ExternalInput").ap()
            for n, v in arrays.items()}
    args["out"] = nc.dram_tensor("out", (1, SEQ, D), F32, kind="ExternalOutput").ap()
    trunk(nc, args)
    r = run_bass_kernel_spmd(nc, [{f"in_{n}": v for n, v in arrays.items()}], core_ids=[0])
    return r.results[0]["out"]
```

```python
from contextlib import ExitStack

import numpy as np

import concourse.bass as bass
from concourse import mybir

ALU = mybir.AluOpType
ACT = mybir.ActivationFunctionType
AX = mybir.AxisListType
F32 = mybir.dt.float32
F32R = mybir.dt.float32r
BF16 = mybir.dt.bfloat16
I32 = mybir.dt.int32

P = 128
DEPTH = 2
D = 1024
SEQ = 256
TT = SEQ // P
KD = D // P
F = 2816
FC = 256
NCH = F // FC
C = 512
CT = C // P
W = 31
H = 8
NOPE, ROPE, VD = 64, 32, 64
QK = NOPE + ROPE
HALF = ROPE // 2
QL = KVL = 256
PR = QL + KVL + ROPE
O1 = 2 * C
O4 = O1 + PR
CHUNK = 64
EPS = 1e-6
SCALE = float(QK) ** -0.5
MASKED = -1e30

UNIT = 4 * PR
RAW = 3
RING = 6
LEAD = 5
U_FFN = 3 * NCH
U_MIX = 24
U_LAYER = 2 * U_FFN + U_MIX
UB = (0, U_FFN + U_MIX)
UM = U_FFN
assert U_LAYER % RING == 0 and U_LAYER % RAW == 0

M_PR, M_C01, M_UQ, M_UKV, M_C23, M_G, M_MLA, M_CO, M_WO = 0, 2, 4, 5, 6, 8, 16, 18, 20

USED = [2048] * U_LAYER
USED[UM + M_PR] = USED[UM + M_PR + 1] = 4 * PR
USED[UM + M_UQ] = 2 * H * QK

D_TAPS = 5
EARLY_TAPS = (4, 4, 8)
P_TAP = sum(EARLY_TAPS) + 2 * D_TAPS - 1
assert sum(EARLY_TAPS) % 2 == 0
N_TAP = CT // 2 * W + D_TAPS + CT
P_FIRST = (0, D_TAPS)
E1, E2 = 3, 7
ACT_TAPS = (range(E2 + 6, W, 4), range(D_TAPS, W, 4))
N_ACT = 2 * (len(ACT_TAPS[0]) + len(ACT_TAPS[1]))
N_PTAP_0 = 2 * W - 1 - 2 * len(ACT_TAPS[0])
N_PTAP = N_PTAP_0 + 2 * (W - D_TAPS) - 2 * len(ACT_TAPS[1])
N_ROPE = 36
N_ROT = 15

V_W = 0
V_CB = CT * W
V_LG = V_CB + CT
V_LB = V_LG + CT
V_CQ = V_LB + CT
V_CKV = V_CQ + 2
V_QK = V_CKV + 2
V_N = V_QK + 2


def unit_gu(f, c, h):
    if isinstance(c, int) and c == 0:
        return UB[f] + h
    return (c - 1) * 3 + (UB[f] + 2 + h)


def unit_down(f, c):
    if isinstance(c, int) and c == NCH - 1:
        return UB[f] + U_FFN - 1
    return c * 3 + (UB[f] + 4)


def two_pi_parts(value, quanta):
    parts = []
    for q in quanta:
        parts.append(float(np.floor(value / q) * q))
        value -= parts[-1]
    return parts + [float(np.float32(value))]


def trunk(nc, a):
    with ExitStack() as ctx:
        def sb(name, shape, dt=F32):
            return ctx.enter_context(nc.sbuf_tensor(name, shape, dt))

        def sem(name):
            return ctx.enter_context(nc.semaphore(name))

        raw = sb("raw", [P, RAW, UNIT])
        whi = sb("whi", [P, RING, UNIT], F32R)
        wlo = sb("wlo", [P, RING, UNIT], F32R)
        x = sb("x", [P, TT, D])
        hThi = sb("hThi", [P, KD, SEQ], F32R)
        hTlo = sb("hTlo", [P, KD, SEQ], F32R)
        gThi = sb("gThi", [P, 4, SEQ], F32R)
        gTlo = sb("gTlo", [P, 4, SEQ], F32R)
        htok = sb("htok", [P, TT * D])
        gain = sb("gain", [P, D])
        gates = sb("gates", [P, TT, 2 * D])
        ktok = sb("ktok", [P, TT, H, QK])
        vtok = sb("vtok", [P, TT, H, VD])
        cu = sb("cu", [P, CT, W - 1 + SEQ])
        cacc = sb("cacc", [P, CT, SEQ])
        qkT = sb("qkT", [P, 2, 2 * SEQ])
        pT = sb("pT", [P, 2, 3 * P])
        bias = sb("bias", [P, C])
        mask = sb("mask", [P, SEQ])
        ident = sb("ident", [P, P])
        mean_of = sb("mean_of", [P, P])
        vec = sb("vec", [P, V_N])
        qkg = sb("qkg", [P, 2, ROPE])
        posi = sb("posi", [P, TT], I32)
        ang = sb("ang", [P, 4, TT, HALF])
        cossin = sb("cossin", [P, 2, TT, HALF])
        small = sb("small", [P, 96 + TT * ROPE])
        expo = sb("expo", [P, 1])
        zero = sb("zero", [P, C], BF16)

        ss = small[:, 0:2]
        ms = small[:, 2:4]
        rs = small[:, 4:6]
        ss4 = small[:, 6:10]
        rs4 = small[:, 10:14]
        ssqk = small[:, 14:46]
        rsqk = small[:, 46:78]
        krope = small[:, 96:96 + TT * ROPE].rearrange("p (t d) -> p t d", t=TT)
        qscale = ssqk[:, 0:16]
        mx = small[:, 78:80]
        nmx = small[:, 80:82]
        psum_h = small[:, 82:84]
        rsum = (small[:, 84:86], small[:, 86:88])
        sgate = gates[:, 0, 0:TT * FC].rearrange("p (t f) -> p t f", t=TT)
        gu = gates[:, 1, 0:TT * FC].rearrange("p (t f) -> p t f", t=TT)
        pr = gates[:, :, 2 * D - PR:2 * D]
        junk = gates[:, :, 0:H * QK]
        qtok = htok[:, 0:TT * H * QK].rearrange("p (t h d) -> p t h d", t=TT, h=H)
        otok = gain[:, :].rearrange("p (t n) -> p t n", t=TT)
        diag = qkT[:, 0, 0:SEQ].rearrange("p (t n) -> p t n", t=TT)
        tail = htok[:, TT * H * QK:TT * D]
        rot = tail.rearrange("p (j t h d) -> p j t h d", j=2, t=TT, h=H)
        prob = tail.rearrange("p (t k) -> p t k", t=TT)
        csq = cu[:, :, W - 1:W - 1 + SEQ]
        prod = [[gates[:, t, 3 * C + i * SEQ:3 * C + (i + 1) * SEQ] for i in range(2)] for t in range(TT)]

        bank = ctx.enter_context(nc.psum_tensor("bank", [P, 8, 512], F32))

        raw_landed = [sem(f"raw_landed{i}") for i in range(RAW)]
        whi_ready = sem("whi_ready")
        wlo_ready = sem("wlo_ready")
        unit_free = sem("unit_free")
        small_landed = sem("small_landed")
        x_landed = [sem(f"x_landed{t}") for t in range(TT)]
        gain_landed = sem("gain_landed")
        bias_landed = sem("bias_landed")
        vec_landed = sem("vec_landed")
        vec_used = sem("vec_used")
        const_ready = sem("const_ready")
        dve_const = sem("dve_const")
        rope_step = sem("rope_step")
        trig_ready = sem("trig_ready")
        x_new = sem("x_new")
        sq_ready = sem("sq_ready")
        ms_ready = sem("ms_ready")
        rs_ready = sem("rs_ready")
        h_ready = sem("h_ready")
        ntr = sem("ntr")
        nhi = sem("nhi")
        nlo = sem("nlo")
        gu_done = sem("gu_done")
        silu_ready = sem("silu_ready")
        gu_ready = sem("gu_ready")
        gtr = sem("gtr")
        ghi = sem("ghi")
        glo = sem("glo")
        acc_done = sem("acc_done")
        pr_done = sem("pr_done")
        pr_ready = sem("pr_ready")
        kr_ready = sem("kr_ready")
        pr_sq = sem("pr_sq")
        pr_ms = sem("pr_ms")
        pr_rs = sem("pr_rs")
        pr_norm = sem("pr_norm")
        lat_tr = sem("lat_tr")
        lat_hi = sem("lat_hi")
        lat_lo = sem("lat_lo")
        tanh_ready = sem("tanh_ready")
        cu_ready = sem("cu_ready")
        q_done = sem("q_done")
        kv_done = sem("kv_done")
        q_ready = sem("q_ready")
        kv_ready = sem("kv_ready")
        qk_sq = sem("qk_sq")
        qk_sum = sem("qk_sum")
        qk_ms = sem("qk_ms")
        qk_rs = sem("qk_rs")
        qk_norm = sem("qk_norm")
        pool_step = sem("pool_step")
        gate_done = sem("gate_done")
        gate_sum = sem("gate_sum")
        gate_ready = sem("gate_ready")
        qkt_done = sem("qkt_done")
        qkt_ready = sem("qkt_ready")
        s_done = sem("s_done")
        max_ready = sem("max_ready")
        nmx_ready = sem("nmx_ready")
        exp_ready = sem("exp_ready")
        rsum_ready = sem("rsum_ready")
        pt_done = sem("pt_done")
        pt_ready = sem("pt_ready")
        pv_done = sem("pv_done")
        o_ready = sem("o_ready")
        ot_done = sem("ot_done")
        ot_hi = sem("ot_hi")
        ot_lo = sem("ot_lo")
        tap = sem("tap")
        pool_tap = sem("pool_tap")
        act_prod = sem("act_prod")
        mean_done = sem("mean_done")
        xc_ready = sem("xc_ready")
        csq_ready = sem("csq_ready")
        var_done = sem("var_done")
        lnv_ready = sem("lnv_ready")
        lnr_ready = sem("lnr_ready")
        diag_ready = sem("diag_ready")
        lnb_done = sem("lnb_done")
        ln_ready = sem("ln_ready")
        act_silu = sem("act_silu")
        c_hi = sem("c_hi")
        c_lo = sem("c_lo")
        mla_done = sem("mla_done")
        ym_ready = sem("ym_ready")
        co_done = sem("co_done")
        yc_ready = sem("yc_ready")
        y_ready = sem("y_ready")
        yt_done = sem("yt_done")
        yt_hi = sem("yt_hi")
        yt_lo = sem("yt_lo")
        stored = sem("stored")

        wg = (a["ffn1_w_gate"], a["ffn2_w_gate"])
        wu = (a["ffn1_w_up"], a["ffn2_w_up"])
        wd = (a["ffn1_w_down"], a["ffn2_w_down"])
        norms = (a["ffn1_norm"], a["mix_norm"], a["ffn2_norm"])

        def unit_waits(eng, l, u):
            eng.wait_ge(wlo_ready, l * U_LAYER + u + (RAW + 1))

        def unit_released(eng, l, u):
            eng.wait_ge(unit_free, l * U_LAYER + u + (RING + 1))

        def per_ffn(l, f, c, t):
            return l * (4 * NCH) + c * TT + (2 * NCH * f + t + 1)

        def per_norm(l, n, t):
            return l * (3 * TT) + (n * TT + t + 1)

        def per_norm_half(l, n, t, h):
            return l * (6 * TT) + ((n * TT + t) * 2 + h + 1)

        def slot(u, n):
            return u % n

        def view(t, u0, n, k):
            return t[:, slot(u0, RING), 0:n].rearrange("p (k n) -> p k n", k=k)

        block = ctx.enter_context(nc.Block())

        def chunks(eng, f, first, pair, last):
            first()
            with eng.Fori(0, (NCH - 3) // 2) as i:
                pair(i * 2 + 1, 1)
                pair(i * 2 + 2, 2)
            last()

        @block.sync
        def _(sp):
            def place(l, u, u0, pairs):
                sp.wait_ge(wlo_ready, l * U_LAYER + u + 1)
                for dst, src in pairs:
                    sp.dma_start(dst, src).then_inc(raw_landed[slot(u0, RAW)], 16)

            def gate_up(l, f, c, c0, h):
                u0 = unit_gu(f, c0, h)
                dst = raw[:, slot(u0, RAW), 0:2048].rearrange("p (k g n) -> p k g n", k=4, g=2)
                rows = slice(4 * h * P, 4 * (h + 1) * P)
                cols = bass.ds(c * FC, FC)
                place(l, unit_gu(f, c, h), u0, [
                    (dst[:, :, g, :], w[l, rows, cols].rearrange("(k p) n -> p k n", p=P))
                    for g, w in enumerate((wg[f], wu[f]))])

            def down(l, f, c, c0):
                u0 = unit_down(f, c0)
                dst = raw[:, slot(u0, RAW), 0:2048].rearrange("p (k n) -> p k n", k=2)
                place(l, unit_down(f, c), u0, [
                    (dst[:, k, :], wd[f][l, bass.ds(c * FC + k * P, P), :]) for k in range(2)])

            def load_gain(l, n):
                sp.wait_ge(h_ready, l * (3 * TT) + (n * TT + 1))
                sp.dma_start(gain[:, :], norms[n][bass.ds(l, 1), :].to_broadcast([P, D])).then_inc(gain_landed, 16)

            def ffn(l, f):
                def first():
                    gate_up(l, f, 0, 0, 0)
                    if f == 0:
                        load_gain(l, 0)
                    gate_up(l, f, 0, 0, 1)

                def pair(c, c0):
                    gate_up(l, f, c, c0, 0)
                    gate_up(l, f, c, c0, 1)
                    down(l, f, c - 1, c0 - 1)

                def last():
                    for c in (NCH - 2, NCH - 1):
                        pair(c, c)
                    down(l, f, NCH - 1, NCH - 1)

                chunks(sp, f, first, pair, last)

            def block_of(l, u, w, r0, k, c0, n):
                dst = raw[:, slot(u, RAW), 0:k * n].rearrange("p (k n) -> p k n", k=k)
                src = w[l, r0:r0 + k * P, c0:c0 + n].rearrange("(k p) n -> p k n", p=P)
                h = k // 2
                place(l, u, u, [(dst[:, h:k], src[:, h:k]), (dst[:, 0:h], src[:, 0:h])])

            sp.dma_start(x[:, 0, :], a["x"][0, 0:P, :]).then_inc(x_landed[0], 16)

            with sp.Fori(0, DEPTH) as l:
                ffn(l, 0)
                load_gain(l, 1)
                sp.wait_ge(vec_used, l + 1)
                sp.dma_start(vec[:, :], a["vec"][l]).then_inc(vec_landed, 16)
                for n, w in enumerate((a["q_norm"], a["k_norm"])):
                    sp.dma_start(qkg[:, n, :], w[bass.ds(l, 1), NOPE:QK].to_broadcast([P, ROPE])).then_inc(vec_landed, 16)
                for h in range(2):
                    block_of(l, UM + M_PR + h, a["w_in"], 4 * h * P, 4, O1, PR)
                def conv_units(base, j):
                    for g in range(2):
                        block_of(l, UM + base + g, a["w_in"], 0, KD, g * C + j * 256, 256)

                conv_units(M_C01, 0)
                block_of(l, UM + M_UQ, a["w_uq"], 0, 2, 0, H * QK)
                block_of(l, UM + M_UKV, a["w_ukv"], 0, 2, 0, H * (NOPE + VD))
                conv_units(M_C23, 1)
                for g in range(4):
                    for h in range(2):
                        block_of(l, UM + M_G + 2 * g + h, a["w_in"], 4 * h * P, 4, O4 + g * C, C)
                for h in range(2):
                    block_of(l, UM + M_MLA + h, a["w_mla_out"], 2 * h * P, 2, 0, D)
                for h in range(2):
                    block_of(l, UM + M_CO + h, a["w_conv_out"], 2 * h * P, 2, 0, D)
                for h in range(4):
                    block_of(l, UM + M_WO + h, a["w_out"], 2 * h * P, 2, 0, D)
                ffn(l, 1)

            for t in range(TT):
                sp.wait_ge(x_new, TT + 6 * DEPTH - (TT - 1 - t))
                sp.dma_start(a["out"][0, t * P:(t + 1) * P, :], x[:, t, :]).then_inc(stored, 16)
            sp.wait_ge(gain_landed, 16 * 3 * DEPTH)
            sp.wait_ge(stored, 16 * TT)

        @block.gpsimd
        def _(pool):
            nc.gpsimd.memset(ident[:, :], 0.0).then_inc(const_ready, 1)
            nc.gpsimd.memset(expo[:, :], -0.5).then_inc(const_ready, 1)
            nc.gpsimd.memset(mean_of[:, :], 1.0 / C).then_inc(const_ready, 1)
            pool.wait_ge(const_ready, 3)
            nc.gpsimd.affine_select(out=ident[:, :], in_=ident[:, :], compare_op=ALU.not_equal, fill=1.0,
                                    base=0, pattern=[[-1, P]], channel_multiplier=1).then_inc(const_ready, 1)

            def root(out, in_):
                return nc.gpsimd.tensor_tensor(out, in_, expo[:, :].to_broadcast([P, out.shape[-1]]), ALU.pow)

            def norm(l, n):
                for t in range(TT):
                    pool.wait_ge(ms_ready, per_norm(l, n, t))
                    root(rs[:, t:t + 1], ms[:, t:t + 1]).then_inc(rs_ready, 1)

            with pool.Fori(0, DEPTH) as l:
                norm(l, 0)
                rstep = [0]

                def r(ins):
                    rstep[0] += 1
                    ins.then_inc(rope_step, 1)
                    pool.wait_ge(rope_step, l * N_ROPE + rstep[0])
                    nc.gpsimd.tensor_tensor(small[:, 95:96], expo[:, :], expo[:, :], ALU.mult)

                A, B2, KH, K2 = (ang[:, i, :, :] for i in range(4))
                pool.wait_ge(small_landed, 16 * TT)
                freq = [float(np.float32(10000.0) ** np.float32(-i / ROPE)) for i in range(0, ROPE, 2)]
                r(nc.gpsimd.tensor_copy(small[:, 91:93], posi[:, :]))
                for i in range(HALF):
                    ins = nc.gpsimd.tensor_scalar(ang[:, 0, :, i], small[:, 91:93], freq[i], None, ALU.mult)
                r(ins)
                two_pi = 2 * np.pi
                big = 65536.0
                magic = 1.5 * 2 ** 23

                def turns(out, period):
                    r(nc.gpsimd.tensor_scalar(out, A, 1.0 / period, magic, ALU.mult, ALU.add))
                    r(nc.gpsimd.tensor_scalar(out, out, magic, None, ALU.subtract))

                def less(k, part):
                    r(nc.gpsimd.tensor_scalar(B2, k, part, None, ALU.mult))
                    r(nc.gpsimd.tensor_tensor(A, A, B2, ALU.subtract))

                parts_big = two_pi_parts(two_pi * big, (2.0 ** 11, 2.0 ** 3, 2.0 ** -5))
                parts = two_pi_parts(two_pi, (2.0 ** -5, 2.0 ** -13, 2.0 ** -21))
                turns(KH, two_pi * big)
                for part in parts_big[:3]:
                    less(KH, part)
                turns(K2, two_pi)
                for part in parts:
                    less(K2, part)
                less(KH, parts_big[3])
                turns(K2, two_pi)
                for part in parts:
                    less(K2, part)
                lim = float(np.nextafter(np.float32(np.pi), np.float32(0)))
                r(nc.gpsimd.tensor_scalar(A, A, lim, -lim, ALU.min, ALU.max))
                r(nc.gpsimd.tensor_scalar(KH, A, 0.0, -2.0, ALU.min, ALU.mult))
                r(nc.gpsimd.tensor_tensor(KH, KH, A, ALU.add))
                r(nc.gpsimd.tensor_scalar(B2, KH, -1.0, float(np.float32(np.pi / 2)), ALU.mult, ALU.add))
                assert rstep[0] == N_ROPE
                norm(l, 1)
                pool.wait_ge(pr_ms, l + 1)
                root(rs4, ss4).then_inc(pr_rs, 1)
                pool.wait_ge(vec_landed, (l + 1) * 48)
                pool.wait_ge(trig_ready, (l + 1) * 2)
                pool.wait_ge(pr_ready, (l + 1) * 2)
                steps = 0

                def step(ins):
                    nonlocal steps
                    steps += 1
                    ins.then_inc(pool_step, 1)

                def seen():
                    pool.wait_ge(pool_step, l * N_ROT + steps)

                def rotate(lo, hi, cos, sin, r0, r1):
                    step(nc.gpsimd.tensor_tensor(r0, hi, sin, ALU.mult))
                    step(nc.gpsimd.tensor_tensor(r1, lo, sin, ALU.mult))
                    seen()
                    step(nc.gpsimd.tensor_tensor(lo, lo, cos, ALU.mult))
                    step(nc.gpsimd.tensor_tensor(hi, hi, cos, ALU.mult))
                    seen()
                    step(nc.gpsimd.tensor_tensor(lo, lo, r0, ALU.subtract))
                    step(nc.gpsimd.tensor_tensor(hi, hi, r1, ALU.add))

                kr = ktok[:, :, 0, NOPE:QK]
                step(nc.gpsimd.tensor_tensor(kr, krope, qkg[:, 1:2, :].to_broadcast([P, TT, ROPE]),
                                             ALU.mult))
                seen()
                rotate(kr[:, :, 0:HALF], kr[:, :, HALF:ROPE], cossin[:, 0], cossin[:, 1], rot[:, 0, :, 0, :],
                       rot[:, 1, :, 0, :])
                done = acts = 0

                def conv(ins):
                    nonlocal done
                    done += 1
                    ins.then_inc(pool_tap, 1)

                def conv_seen():
                    pool.wait_ge(pool_tap, l * N_PTAP + done)

                def product(ct, out, k):
                    w = vec[:, V_W + ct * W + k:V_W + ct * W + k + 1]
                    conv(nc.gpsimd.tensor_tensor(out, cu[:, ct, k:k + SEQ], w.to_broadcast([P, SEQ]), ALU.mult))

                def tap_pairs(j, ks):
                    nonlocal acts
                    ct = 2 * j + 1
                    for k in ks:
                        by_act = k in ACT_TAPS[j]
                        slots = prod[1 if by_act else 0]
                        if by_act:
                            acts += 2
                        else:
                            conv_seen()
                            for i in range(2):
                                product(ct, slots[i], k + i)
                        for i in range(2):
                            if by_act and i == 0:
                                pool.wait_ge(act_prod, l * N_ACT + acts)
                            conv_seen()
                            conv(nc.gpsimd.tensor_tensor(cacc[:, ct, :], cacc[:, ct, :], slots[i], ALU.add))

                pool.wait_ge(lat_tr, (l + 1) * 2)
                pool.wait_ge(cu_ready, l * 2 + 1)
                product(1, cacc[:, 1, :], 0)
                tap_pairs(0, range(1, E1, 2))
                pool.wait_ge(qk_sq, l * 2 + 1)
                for t in range(TT):
                    step(nc.gpsimd.tensor_tensor(qtok[:, t, :, NOPE:QK], qtok[:, t, :, NOPE:QK],
                                                 qkg[:, 0:1, :].to_broadcast([P, H, ROPE]), ALU.mult))
                seen()
                rotate(qtok[:, :, :, NOPE:NOPE + HALF], qtok[:, :, :, NOPE + HALF:QK],
                       *(cossin[:, i].unsqueeze(2).to_broadcast([P, TT, H, HALF]) for i in range(2)),
                       rot[:, 0], rot[:, 1])
                assert steps == N_ROT
                pool.wait_ge(qk_ms, l * 2 + 1)
                root(rsqk[:, 0:16], ssqk[:, 0:16]).then_inc(qk_rs, 1)
                tap_pairs(0, range(E1, E2, 2))
                pool.wait_ge(qk_ms, l * 2 + 2)
                root(rsqk[:, 16:32], ssqk[:, 16:32]).then_inc(qk_rs, 1)
                tap_pairs(0, range(E2, W, 2))
                pool.wait_ge(tap, l * N_TAP + P_TAP)
                tap_pairs(1, range(D_TAPS, W, 2))
                assert done == N_PTAP
                pool.wait_ge(lnv_ready, l + 1)
                root(rs, ms).then_inc(lnr_ready, 1)
                norm(l, 2)

        @block.tensor
        def _(pe):
            def products(out, lhs, rhs, start, stop, skip=False):
                (lh, ll), (rh, rl) = lhs, rhs
                nc.tensor.matmul(out, lh, rh, start=start, stop=False, skip_group_check=skip)
                nc.tensor.matmul(out, lh, rl, start=False, stop=False, skip_group_check=skip)
                return nc.tensor.matmul(out, ll, rh, start=False, stop=stop, skip_group_check=skip)

            def keep_busy(n):
                for _ in range(n):
                    nc.tensor.matmul(bank[:, 4, :], zero[:, 0:P], zero[:, :], start=True, stop=True)

            def hT(k, t=None):
                s = slice(0, SEQ) if t is None else slice(t * P, (t + 1) * P)
                return hThi[:, k, s], hTlo[:, k, s]

            def gT(k, t):
                return gThi[:, k, t * P:(t + 1) * P], gTlo[:, k, t * P:(t + 1) * P]

            def wt(u0, n, k, row, cols):
                return view(whi, u0, n, k)[:, row, cols], view(wlo, u0, n, k)[:, row, cols]

            def norm(l, n, t):
                if n == 0 and t == 0:
                    keep_busy(12)
                pe.wait_ge(h_ready, l * (3 * TT) + (n * TT + t + 2))
                for h in range(2):
                    if t:
                        pe.wait_ge(nlo, per_norm_half(l, n, 0, h))
                    for k in range(4):
                        o = t * D + (4 * h + k) * P
                        ins = nc.tensor.transpose(bank[:, 6 + h, k * P:(k + 1) * P], htok[:, o:o + P], ident[:, :])
                    ins.then_inc(ntr, 1)
                if n == 0 and t == 0:
                    keep_busy(5)

            def ffn(l, f):
                n = 2 * f

                def gate_up(c, c0, t):
                    if not isinstance(c, int) or c > 0:
                        pe.wait_ge(gu_ready, per_ffn(l, f, c - 1, t))
                    for h in range(2):
                        if isinstance(c, int) and c == 0:
                            pe.wait_ge(nlo, per_norm_half(l, n, t, h))
                        if t == 0:
                            unit_waits(pe, l, unit_gu(f, c, h))
                        for k in range(4):
                            ins = products(bank[:, 4 + t, :], hT(4 * h + k, t),
                                           wt(unit_gu(f, c0, h), 2048, 4, k, slice(0, 2 * FC)),
                                           start=(h == 0 and k == 0), stop=(h == 1 and k == 3))
                        if t == 1:
                            ins.then_inc(unit_free, 1)
                        elif h == 1:
                            ins.then_inc(gu_done, 1)

                def turn(c, t):
                    pe.wait_ge(gu_ready, per_ffn(l, f, c, t))
                    if isinstance(c, int) and c == 0:
                        pe.wait_ge(nlo, per_norm_half(l, n, 1, 1))
                    else:
                        pe.wait_ge(glo, per_ffn(l, f, c - 1, t))
                    for k in range(2):
                        ins = nc.tensor.transpose(bank[:, 6 + t, k * P:(k + 1) * P], gu[:, t, k * P:(k + 1) * P],
                                                  ident[:, :])
                    ins.then_inc(gtr, 1)

                def down(c, c0, t, last=False):
                    pe.wait_ge(glo, per_ffn(l, f, c, t))
                    if t == 0:
                        unit_waits(pe, l, unit_down(f, c))
                    for k in range(2):
                        for m in range(2):
                            ins = products(bank[:, 2 * t + m, :], gT((c0 % 2) * 2 + k, t),
                                           wt(unit_down(f, c0), 2048, 2, k, slice(m * 512, (m + 1) * 512)),
                                           start=False, stop=last and k == 1, skip=True)
                    if t == 1:
                        ins.then_inc(unit_free, 1)
                    elif last:
                        ins.then_inc(acc_done, 1)

                def first():
                    if f == 0:
                        norm(l, n, 0)
                    gate_up(0, 0, 0)
                    norm(l, n, 1)
                    for b in range(4):
                        nc.tensor.matmul(bank[:, b, :], zero[:, 0:P], zero[:, :], start=True, stop=False,
                                         skip_group_check=True)
                    gate_up(0, 0, 1)
                    turn(0, 0)

                def pair(c, c0):
                    gate_up(c, c0, 0)
                    turn(c - 1, 1)
                    gate_up(c, c0, 1)
                    down(c - 1, c0 - 1, 0)
                    turn(c, 0)
                    down(c - 1, c0 - 1, 1)

                def last():
                    pair(NCH - 2, NCH - 2)
                    c = NCH - 1
                    gate_up(c, c, 0)
                    turn(c - 1, 1)
                    gate_up(c, c, 1)
                    turn(c, 0)
                    down(c - 1, c - 1, 0)
                    turn(c, 1)
                    down(c, c, 0, last=True)
                    down(c - 1, c - 1, 1)
                    down(c, c, 1, last=True)

                chunks(pe, f, first, pair, last)

            def latents_turn(l):
                for j in range(2):
                    pe.wait_ge(pr_norm, l + 1)
                    for k in range(2):
                        for t in range(TT):
                            o = (k * TT + t) * P
                            ins = nc.tensor.transpose(bank[:, 6 + j, o:o + P],
                                                      pr[:, t, (2 * j + k) * P:(2 * j + k + 1) * P], ident[:, :])
                    ins.then_inc(lat_tr, 1)

            def conv_in(l, j, base, b0, between=None):
                for g in range(2):
                    u = UM + base + g
                    unit_waits(pe, l, u)
                    for ct in range(2):
                        if between and (g, ct) == (1, 0):
                            between(l)
                        for k in range(KD):
                            ins = products(bank[:, b0 + g, ct * SEQ:(ct + 1) * SEQ],
                                           wt(u, 2048, KD, k, slice(ct * P, (ct + 1) * P)), hT(k),
                                           start=(k == 0), stop=(k == KD - 1))
                    ins.then_inc(unit_free, 1)

            def head_turn(l, h):
                if h == 0:
                    pe.wait_ge(pool_step, (l + 1) * N_ROT)
                    pe.wait_ge(qk_norm, (l + 1) * 2)
                else:
                    pe.wait_ge(qkt_ready, l * (2 * H) + 2 * h)
                for j, tok in enumerate((qtok, ktok)):
                    for t in range(TT):
                        o = j * SEQ + t * P
                        ins = nc.tensor.transpose(bank[0:QK, 4, o:o + P], tok[:, t, h, :], ident[:, :])
                ins.then_inc(qkt_done, 1)

            def head_scores(l, h):
                pe.wait_ge(qkt_ready, l * (2 * H) + 2 * h + 2)
                if h:
                    pe.wait_ge(max_ready, l * (2 * H) + 2 * h)
                q = qkT[0:QK, h % 2, :]
                nc.tensor.matmul(bank[:, 5, 0:P], q[:, 0:P], q[:, SEQ:SEQ + P], start=True, stop=True)
                nc.tensor.matmul(bank[:, 5, P:3 * P], q[:, P:2 * P], q[:, SEQ:2 * SEQ], start=True,
                                 stop=True).then_inc(s_done, 1)

            def head_probs(l, h):
                pe.wait_ge(exp_ready, l * H + h + 1)
                if h:
                    pe.wait_ge(pt_ready, l * H + h)
                nc.tensor.transpose(bank[:, 6, 0:P], prob[:, 0, 0:P], ident[:, :])
                nc.tensor.transpose(bank[:, 6, P:2 * P], prob[:, 1, 0:P], ident[:, :])
                nc.tensor.transpose(bank[:, 6, 2 * P:3 * P], prob[:, 1, P:2 * P], ident[:, :]).then_inc(pt_done, 1)

            def head_values(l, h):
                pe.wait_ge(pt_ready, l * H + h + 1)
                if h:
                    pe.wait_ge(o_ready, l * H + h)
                p = pT[:, h % 2, :]
                nc.tensor.matmul(bank[:, 7, 0:VD], p[:, 0:P], vtok[:, 0, h, :], start=True, stop=True)
                nc.tensor.matmul(bank[:, 7, VD:2 * VD], p[:, P:2 * P], vtok[:, 0, h, :], start=True, stop=False)
                nc.tensor.matmul(bank[:, 7, VD:2 * VD], p[:, 2 * P:3 * P], vtok[:, 1, h, :], start=False,
                                 stop=True).then_inc(pv_done, 1)

            def rows_out(l, u, units, lhs, t, b0, done, between={}):
                for i in range(units):
                    if i in between:
                        between[i]()
                    if t == 0:
                        unit_waits(pe, l, u + i)
                    for k in range(2):
                        for m in range(2):
                            ins = products(bank[:, b0 + m, :], lhs(2 * i + k, t),
                                           wt(u + i, 2048, 2, k, slice(m * 512, (m + 1) * 512)),
                                           start=(i == 0 and k == 0), stop=(i == units - 1 and k == 1))
                    if t == 1:
                        ins.then_inc(unit_free, 1)
                    elif i == units - 1:
                        ins.then_inc(done, 1)

            def mean(l):
                pe.wait_ge(tap, (l + 1) * N_TAP)
                pe.wait_ge(gate_sum, l * 8 + 6)
                for ct in range(CT):
                    ins = nc.tensor.matmul(bank[:, 3, 0:SEQ], mean_of[:, :], cacc[:, ct, :], start=(ct == 0),
                                           stop=(ct == CT - 1))
                ins.then_inc(mean_done, 1)

            def mixer(l):
                for t in range(TT):
                    norm(l, 1, t)
                    for h in range(2):
                        u = UM + M_PR + h
                        if t == 0:
                            unit_waits(pe, l, u)
                        pe.wait_ge(nlo, per_norm_half(l, 1, t, h))
                        for k in range(4):
                            for m in range(2):
                                ins = products(bank[:, 2 * t + m, 0:PR // 2], hT(4 * h + k, t),
                                               wt(u, 4 * PR, 4, k, slice(m * PR // 2, (m + 1) * PR // 2)),
                                               start=(h == 0 and k == 0), stop=(h == 1 and k == 3))
                        if t == 1:
                            ins.then_inc(unit_free, 1)
                        elif h == 1:
                            ins.then_inc(pr_done, 1)
                conv_in(l, 0, M_C01, 4, between=latents_turn)
                for t in range(TT):
                    if t == 0:
                        unit_waits(pe, l, UM + M_UQ)
                        pe.wait_ge(lat_lo, l * 4 + 2)
                    for k in range(2):
                        for m in range(2):
                            ins = products(bank[:, 2 * t + m, 0:4 * QK], gT(k, t),
                                           wt(UM + M_UQ, 2 * H * QK, 2, k, slice(m * 4 * QK, (m + 1) * 4 * QK)),
                                           start=(k == 0), stop=(k == 1))
                    ins.then_inc(unit_free if t else q_done, 1)
                for t in range(TT):
                    if t == 0:
                        unit_waits(pe, l, UM + M_UKV)
                        pe.wait_ge(lat_lo, l * 4 + 4)
                        pe.wait_ge(cu_ready, l * 2 + 1)
                    for k in range(2):
                        for m in range(2):
                            ins = products(bank[:, 4 + 2 * t + m, :], gT(2 + k, t),
                                           wt(UM + M_UKV, 2048, 2, k, slice(m * 512, (m + 1) * 512)),
                                           start=(k == 0), stop=(k == 1))
                    ins.then_inc(unit_free if t else kv_done, 1)
                pe.wait_ge(q_ready, l * 4 + 2)
                conv_in(l, 1, M_C23, 0)
                for u8 in range(8):
                    g, kh = u8 // 2, u8 % 2
                    b0 = 2 if g % 2 == 0 else 0
                    u = UM + M_G + u8
                    if u8 == 0:
                        pe.wait_ge(kv_ready, l * 8 + 8)
                    if u8 > 1:
                        head_turn(l, u8 - 1)
                    for t in range(TT):
                        if u8 == 1 and t == 1:
                            head_turn(l, 0)
                        if t == 0:
                            unit_waits(pe, l, u)
                        if kh == 0:
                            if g == 0:
                                pe.wait_ge(q_ready, l * 4 + 4)
                            elif g == 1:
                                pe.wait_ge(cu_ready, l * 2 + 2)
                            else:
                                pe.wait_ge(gate_sum, l * 8 + ((g - 2) * 2 + t + 1))
                        for k in range(4):
                            ins = products(bank[:, b0 + t, :], hT(4 * kh + k, t), wt(u, 2048, 4, k, slice(0, 512)),
                                           start=(kh == 0 and k == 0), stop=(kh == 1 and k == 3))
                        if t == 1:
                            ins.then_inc(unit_free, 1)
                        elif kh == 1:
                            ins.then_inc(gate_done, 1)
                        if t == 0 and u8 > 1:
                            head_probs(l, u8 - 2)
                        if (t == 0 and u8 > 1) or (t == 1 and u8 == 1):
                            head_scores(l, u8 - 1)
                        if t == 0 and u8 == 7:
                            head_turn(l, H - 1)
                    if u8 >= 2:
                        head_values(l, u8 - 2)
                head_scores(l, H - 1)
                head_probs(l, H - 2)
                head_values(l, H - 2)
                head_probs(l, H - 1)
                mean(l)
                head_values(l, H - 1)
                for t in range(TT):
                    if t == 0:
                        pe.wait_ge(o_ready, (l + 1) * H)
                    for k in range(4):
                        ins = nc.tensor.transpose(bank[:, 4 + t, k * P:(k + 1) * P], otok[:, t, k * P:(k + 1) * P],
                                                  ident[:, :])
                    ins.then_inc(ot_done, 1)
                def variance():
                    pe.wait_ge(csq_ready, l + 1)
                    for t in range(TT):
                        for ct in range(CT):
                            ins = nc.tensor.matmul(bank[:, 6, SEQ + t:SEQ + t + 1], csq[:, ct, t * P:(t + 1) * P],
                                                   mean_of[:, 0:1], start=(ct == 0), stop=(ct == CT - 1))
                    ins.then_inc(var_done, 1)

                def root_rows():
                    pe.wait_ge(diag_ready, (l + 1) * TT)
                    nc.tensor.matmul(bank[:, 6, 0:SEQ], mean_of[:, :], qkT[:, 0, 0:SEQ], start=True,
                                     stop=True).then_inc(lnb_done, 1)

                variance()
                pe.wait_ge(xc_ready, l + 1)
                for t in range(TT):
                    pe.wait_ge(ot_lo, l * 2 + t + 1)
                    pe.wait_ge(gate_sum, l * 8 + (6 if t == 0 else 8))
                    rows_out(l, UM + M_MLA, 2, hT, t, 2 - 2 * t, mla_done, between={1: root_rows} if t == 0 else {})
                pe.wait_ge(c_lo, l + 1)
                def y_turn(t):
                    for h in range(2):
                        pe.wait_ge(y_ready, l * 4 + t * 2 + h + 1)
                        for k in range(4):
                            o = (4 * h + k) * P
                            ins = nc.tensor.transpose(bank[:, 2 * t + h, k * P:(k + 1) * P], gates[:, t, o:o + P],
                                                      ident[:, :])
                        ins.then_inc(yt_done, 1)

                rows_out(l, UM + M_CO, 2, gT, 0, 4, co_done)
                rows_out(l, UM + M_CO, 2, gT, 1, 6, co_done, between={1: lambda: y_turn(0)})
                pe.wait_ge(yt_lo, l * 4 + 2)
                rows_out(l, UM + M_WO, 4, hT, 0, 4, acc_done, between={3: lambda: y_turn(1)})
                pe.wait_ge(yt_lo, l * 4 + 4)
                rows_out(l, UM + M_WO, 4, hT, 1, 2, acc_done, between={3: lambda: norm(l, 2, 0)})

            pe.sem_inc(unit_free, RING)
            pe.wait_ge(const_ready, 4)
            pe.wait_ge(dve_const, 1)
            keep_busy(10)
            with pe.Fori(0, DEPTH) as l:
                ffn(l, 0)
                mixer(l)
                ffn(l, 1)


        @block.scalar
        def _(act):
            def split(l, u0, turns=0):
                n = (l * (U_LAYER // RAW) + turns + (u0 // RAW + 1)) * 32
                act.wait_ge(raw_landed[slot(u0, RAW)], n)
                act.wait_ge(unit_free, l * U_LAYER + turns * RAW + (u0 + 1))
                nc.scalar.activation(whi[:, slot(u0, RING), 0:USED[u0]], raw[:, slot(u0, RAW), 0:USED[u0]],
                                     ACT.Copy).then_inc(whi_ready, 1)

            def norm_squares(l, n, t):
                act.wait_ge(x_new, l * 6 + (n * TT + t + 1))
                if n == 0:
                    act.wait_ge(x_landed[t], 16)
                nc.scalar.activation(htok[:, t * D:(t + 1) * D], x[:, t, :], ACT.Square,
                                     accum_out=ss[:, t:t + 1]).then_inc(sq_ready, 1)

            def norm_round(l, n, t):
                for h in range(2):
                    act.wait_ge(ntr, per_norm_half(l, n, t, h))
                    nc.scalar.activation(hThi[:, 4 * h:4 * h + 4, t * P:(t + 1) * P],
                                         bank[:, 6 + h, :].rearrange("p (k n) -> p k n", k=4),
                                         ACT.Copy).then_inc(nhi, 1)

            def ffn(l, f):
                def silu(c, t):
                    if t == 0:
                        act.wait_ge(gu_done, l * (2 * NCH) + c + (NCH * f + 1))
                    else:
                        unit_released(act, l, unit_gu(f, c, 1))
                    nc.scalar.activation(sgate[:, t, :], bank[:, 4 + t, 0:FC], ACT.Silu).then_inc(silu_ready, 1)

                def round_gu(c, c0, t):
                    act.wait_ge(gtr, per_ffn(l, f, c, t))
                    if not (isinstance(c, int) and c == 0):
                        unit_released(act, l, c * 3 + (UB[f] - 2))
                    nc.scalar.activation(gThi[:, (c0 % 2) * 2:(c0 % 2) * 2 + 2, t * P:(t + 1) * P],
                                         bank[:, 6 + t, 0:2 * P].rearrange("p (k n) -> p k n", k=2),
                                         ACT.Copy).then_inc(ghi, 1)

                def first():
                    split(l, UB[f] + 2)
                    silu(0, 0)
                    split(l, UB[f] + 3)
                    silu(0, 1)
                    round_gu(0, 0, 0)
                    split(l, UB[f] + 4)

                def pair(c, c0, i=0):
                    u = UB[f] + 2 + 3 * c0
                    split(l, u, i)
                    silu(c, 0)
                    round_gu(c - 1, c0 - 1, 1)
                    split(l, u + 1, i)
                    silu(c, 1)
                    round_gu(c, c0, 0)
                    split(l, u + 2, i)

                first()
                with act.Fori(0, (NCH - 3) // 2) as i:
                    pair(i * 2 + 1, 1, i * 2)
                    pair(i * 2 + 2, 2, i * 2)
                pair(NCH - 2, NCH - 2)
                c = NCH - 1
                if f == 0:
                    split(l, UB[f] + 2 + 3 * c)
                else:
                    split(l, UB[f] + U_FFN - 1)
                silu(c, 0)
                round_gu(c - 1, c - 1, 1)
                if f == 0:
                    split(l, UB[f] + 3 + 3 * c)
                silu(c, 1)
                round_gu(c, c, 0)
                if f == 0:
                    split(l, UB[f] + 4 + 3 * c)
                round_gu(c, c, 1)

            def mixer(l):
                s = iter(range(UM + LEAD, UM + U_MIX + LEAD))

                def one():
                    split(l, next(s))

                def load_bias(g):
                    act.dma_start(bias[:, :], a["gate_bias"][l, g // 2:g // 2 + 1, (g % 2) * C:(g % 2 + 1) * C]
                                  .to_broadcast([P, C])).then_inc(bias_landed, 16)

                load_bias(0)
                act.wait_ge(rope_step, (l + 1) * N_ROPE)
                for i in range(2):
                    nc.scalar.activation(cossin[:, 1 - i, :, :], ang[:, i, :, :], ACT.Sin).then_inc(trig_ready, 1)
                for t in range(TT):
                    if t == 0:
                        act.wait_ge(pr_done, l + 1)
                    else:
                        unit_released(act, l, UM + M_PR + 1)
                    nc.scalar.activation(krope[:, t, :], bank[:, 2 * t + 1, PR // 2 - ROPE:PR // 2], ACT.Copy)
                    nc.scalar.activation(pr[:, t, :].rearrange("p (m n) -> p m n", m=2),
                                         bank[:, 2 * t:2 * t + 2, 0:PR // 2], ACT.Copy).then_inc(pr_ready, 1)
                    act.wait_ge(pr_ready, l * 2 + t + 1)
                    for j in range(2):
                        nc.scalar.activation(junk[:, t, j * QL:(j + 1) * QL], pr[:, t, j * QL:(j + 1) * QL], ACT.Square,
                                             accum_out=ss4[:, 2 * t + j:2 * t + j + 1]).then_inc(pr_sq, 1)
                one()
                one()
                act.wait_ge(vec_landed, (l + 1) * 48)
                for j in range(2):
                    act.wait_ge(lat_tr, l * 2 + j + 1)
                    for k in range(2):
                        nc.scalar.activation(gThi[:, 2 * j + k, :], bank[:, 6 + j, k * SEQ:(k + 1) * SEQ], ACT.Copy,
                                             scale=vec[:, V_CQ + 2 * j + k:V_CQ + 2 * j + k + 1]).then_inc(lat_hi, 1)
                unit_released(act, l, UM + M_C01 + 1)
                nc.scalar.activation(cacc[:, 0:2, :].rearrange("p c n -> p (c n)"), bank[:, 5, :], ACT.Tanh,
                                     scale=0.5).then_inc(tanh_ready, 1)
                one()
                one()
                for t in range(TT):
                    if t == 0:
                        act.wait_ge(q_done, l + 1)
                    else:
                        unit_released(act, l, UM + M_UQ)
                    for m in range(2):
                        nc.scalar.activation(qtok[:, t, 4 * m:4 * m + 4, :].rearrange("p h d -> p (h d)"),
                                             bank[:, 2 * t + m, 0:4 * QK], ACT.Copy).then_inc(q_ready, 1)
                act.wait_ge(q_ready, (l + 1) * 4)
                nc.scalar.activation(junk, qtok.rearrange("p t h d -> p t (h d)"),
                                     ACT.Square).then_inc(qk_sq, 1)
                one()
                for t in range(TT):
                    if t == 0:
                        act.wait_ge(kv_done, l + 1)
                    else:
                        unit_released(act, l, UM + M_UKV)
                    for m in range(2):
                        kv = bank[:, 4 + 2 * t + m, :].rearrange("p (h d) -> p h d", h=4)
                        nc.scalar.activation(ktok[:, t, 4 * m:4 * m + 4, 0:NOPE], kv[:, :, 0:NOPE],
                                             ACT.Copy).then_inc(kv_ready, 1)
                        nc.scalar.activation(vtok[:, t, 4 * m:4 * m + 4, :], kv[:, :, NOPE:NOPE + VD],
                                             ACT.Copy).then_inc(kv_ready, 1)
                    act.wait_ge(pool_step, l * N_ROT + 7)
                    nc.scalar.activation(ktok[:, t, 1:H, NOPE:QK],
                                         ktok[:, t, 0:1, NOPE:QK].to_broadcast([P, H - 1, ROPE]),
                                         ACT.Copy).then_inc(kr_ready, 1)
                act.wait_ge(kv_ready, (l + 1) * 8)
                act.wait_ge(qk_sum, l * 2 + 1)
                squares = junk.rearrange("p t (h d) -> p t h d", h=H)
                for t in range(TT):
                    nc.scalar.activation(squares[:, t, :, NOPE:QK],
                                         krope[:, t:t + 1, :].to_broadcast([P, H, ROPE]), ACT.Square)
                nc.scalar.activation(squares[:, :, :, 0:NOPE], ktok[:, :, :, 0:NOPE],
                                     ACT.Square).then_inc(qk_sq, 1)
                one()
                unit_released(act, l, UM + M_C23 + 1)
                nc.scalar.activation(cacc[:, 2:4, :].rearrange("p c n -> p (c n)"), bank[:, 1, :], ACT.Tanh,
                                     scale=0.5).then_inc(tanh_ready, 1)
                one()
                one()

                def head_copy(h):
                    act.wait_ge(qkt_done, l * H + h + 1)
                    for j in range(2):
                        nc.scalar.activation(qkT[0:QK, h % 2, j * SEQ:(j + 1) * SEQ],
                                             bank[0:QK, 4, j * SEQ:(j + 1) * SEQ], ACT.Copy,
                                             scale=vec[0:QK, V_QK + j:V_QK + j + 1]).then_inc(qkt_ready, 1)

                def head_exp(h):
                    act.wait_ge(nmx_ready, l * H + h + 1)
                    nc.scalar.activation(prob[:, 0, 0:P], prob[:, 0, 0:P], ACT.Exp, bias=nmx[:, 0:1],
                                         scale=qscale[:, h:h + 1],
                                         accum_out=psum_h[:, 0:1])
                    nc.scalar.activation(prob[:, 1, :], prob[:, 1, :], ACT.Exp, bias=nmx[:, 1:2],
                                         scale=qscale[:, H + h:H + h + 1],
                                         accum_out=psum_h[:, 1:2]).then_inc(exp_ready, 1)

                def head_probs(h):
                    act.wait_ge(pt_done, l * H + h + 1)
                    nc.scalar.activation(pT[:, h % 2, :], bank[:, 6, 0:3 * P], ACT.Copy).then_inc(pt_ready, 1)

                def gate_tanh(g):
                    for t in range(TT):
                        act.wait_ge(gate_sum, l * 8 + (g * 2 + t + 1))
                        o = gates[:, t, g * C:(g + 1) * C]
                        nc.scalar.activation(o, o, ACT.Tanh, scale=0.5).then_inc(gate_ready, 1)
                    if g < 3:
                        load_bias(g + 1)

                pairs = iter([(j, k) for j in range(2) for k in ACT_TAPS[j]])
                last_sum = [None]

                def products():
                    j, k = next(pairs, (None, None))
                    if j is None:
                        return
                    n = (N_PTAP_0 if j else 1) + sum(2 if q in ACT_TAPS[j] else 4
                                                     for q in range(P_FIRST[j] + (j == 0), k, 2))
                    act.wait_ge(cu_ready, l * 2 + j + 1)
                    if last_sum[0] is None:
                        act.wait_ge(lat_tr, (l + 1) * 2)
                    else:
                        act.wait_ge(pool_tap, l * N_PTAP + last_sum[0])
                    last_sum[0] = n + 2
                    ct = 2 * j + 1
                    for i in range(2):
                        nc.scalar.activation(prod[1][i], cu[:, ct, k + i:k + i + SEQ], ACT.Copy,
                                             scale=vec[:, V_W + ct * W + k + i:V_W + ct * W + k + i + 1]
                                             ).then_inc(act_prod, 1)

                def load_tables(function, column):
                    nc.scalar.activation(small[:, column:column + 1], expo[:, :], function)

                load_tables(ACT.Exp, 88)
                for u8 in range(8):
                    if u8 >= 1 and u8 != 2:
                        head_copy(u8 - 1)
                    if u8 == 1:
                        head_exp(0)
                        head_copy(1)
                    if u8 == 2:
                        products()
                    one()
                    if u8 >= 2:
                        head_probs(u8 - 2)
                    if u8 % 2 == 0 and u8:
                        gate_tanh(u8 // 2 - 1)
                    products()
                    if u8 == 7:
                        head_copy(H - 1)
                    if u8 > 1:
                        head_exp(u8 - 1)
                    if u8 > 1:
                        products()
                assert next(pairs, None) is None
                head_probs(H - 2)
                head_exp(H - 1)
                head_probs(H - 1)
                act.wait_ge(xc_ready, l + 1)
                nc.scalar.activation(csq, cacc[:, :, :], ACT.Square).then_inc(csq_ready, 1)
                for t in range(TT):
                    act.wait_ge(ot_done, l * 2 + t + 1)
                    nc.scalar.activation(hThi[:, 0:4, t * P:(t + 1) * P],
                                         bank[:, 4 + t, :].rearrange("p (k n) -> p k n", k=4),
                                         ACT.Copy).then_inc(ot_hi, 1)
                gate_tanh(3)
                one()
                act.dma_start(gain[:, :], norms[2][bass.ds(l, 1), :].to_broadcast([P, D])).then_inc(gain_landed, 16)
                load_tables(ACT.Silu, 89)
                act.wait_ge(ln_ready, l + 1)
                for ct in range(CT):
                    nc.scalar.activation(cacc[:, ct, :], cacc[:, ct, :], ACT.Silu,
                                         scale=vec[:, V_LG + ct:V_LG + ct + 1],
                                         bias=vec[:, V_LB + ct:V_LB + ct + 1]).then_inc(act_silu, 1)
                act.wait_ge(act_silu, (l + 1) * CT)
                nc.scalar.activation(gThi[:, :, :], cacc[:, :, :], ACT.Copy).then_inc(c_hi, 1)
                one()
                one()
                for t in range(TT):
                    for h in range(2):
                        act.wait_ge(yt_done, l * 4 + t * 2 + h + 1)
                        nc.scalar.activation(hThi[:, 4 * h:4 * h + 4, t * P:(t + 1) * P],
                                             bank[:, 2 * t + h, :].rearrange("p (k n) -> p k n", k=4),
                                             ACT.Copy).then_inc(yt_hi, 1)
                    if t == 0:
                        one()
                        one()
                assert next(s) == UB[1] + 2

            for t in range(TT):
                act.dma_start(posi[:, t:t + 1], a["positions"][0, t * P:(t + 1) * P].unsqueeze(1)
                              ).then_inc(small_landed, 16)
            act.wait_ge(x_landed[0], 16)
            act.dma_start(x[:, 1, :], a["x"][0, P:SEQ, :]).then_inc(x_landed[1], 16)
            with act.Fori(0, DEPTH) as l:
                for n, (stage, lead) in enumerate(((lambda: ffn(l, 0), 0), (lambda: mixer(l), UM),
                                                   (lambda: ffn(l, 1), UB[1]))):
                    for t in range(TT):
                        norm_squares(l, n, t)
                        if n == 0 and t == 0:
                            split(l, 0)
                        norm_round(l, n, t)
                        if n == 0 and t == 0:
                            split(l, 1)
                    if n == 1:
                        for u in range(lead + 2, lead + LEAD):
                            split(l, u)
                    stage()

        @block.vector
        def _(dve):
            def split(l, u0, turns=0):
                dve.wait_ge(whi_ready, l * U_LAYER + turns * RAW + (u0 + 1))
                n = USED[u0]
                nc.vector.tensor_tensor(wlo[:, slot(u0, RING), 0:n], raw[:, slot(u0, RAW), 0:n],
                                        whi[:, slot(u0, RING), 0:n].bitcast(F32),
                                        ALU.subtract).then_inc(wlo_ready, 1)

            def rest(out, in_, hi):
                return nc.vector.tensor_tensor(out, in_, hi.bitcast(F32), ALU.subtract)

            def norm_scale(l, n, t):
                dve.wait_ge(sq_ready, per_norm(l, n, t))
                nc.vector.tensor_scalar(ms[:, t:t + 1], ss[:, t:t + 1], 1.0 / D, EPS, ALU.mult,
                                        ALU.add).then_inc(ms_ready, 1)

            def norm_apply(l, n, t):
                dve.wait_ge(rs_ready, per_norm(l, n, t))
                if t == 0:
                    dve.wait_ge(gain_landed, l * 48 + 16 * (n + 1))
                nc.vector.scalar_tensor_tensor(out=htok[:, t * D:(t + 1) * D], in0=x[:, t, :],
                                               scalar=rs[:, t:t + 1], in1=gain[:, :], op0=ALU.mult,
                                               op1=ALU.mult).then_inc(h_ready, 1)

            def norm_rest(l, n, t):
                for h in range(2):
                    dve.wait_ge(nhi, per_norm_half(l, n, t, h))
                    rest(hTlo[:, 4 * h:4 * h + 4, t * P:(t + 1) * P],
                         bank[:, 6 + h, :].rearrange("p (k n) -> p k n", k=4),
                         hThi[:, 4 * h:4 * h + 4, t * P:(t + 1) * P]).then_inc(nlo, 1)

            def residual(l, stage, t, b0, u_last):
                if t == 0:
                    dve.wait_ge(acc_done, l * 3 + stage + 1)
                else:
                    unit_released(dve, l, u_last)
                nc.vector.scalar_tensor_tensor(out=x[:, t, :], in0=bank[:, b0:b0 + 2, :].rearrange("p b n -> p (b n)"),
                                               scalar=0.5, in1=x[:, t, :], op0=ALU.mult,
                                               op1=ALU.add).then_inc(x_new, 1)

            def ffn(l, f):
                def mul(c, t):
                    dve.wait_ge(silu_ready, per_ffn(l, f, c, t))
                    if not (isinstance(c, int) and c == 0):
                        dve.wait_ge(gtr, per_ffn(l, f, c - 1, t))
                    nc.vector.tensor_tensor(gu[:, t, :], sgate[:, t, :], bank[:, 4 + t, FC:2 * FC],
                                            ALU.mult).then_inc(gu_ready, 1)

                def rest_gu(c, c0, t):
                    dve.wait_ge(ghi, per_ffn(l, f, c, t))
                    o = gThi[:, (c0 % 2) * 2:(c0 % 2) * 2 + 2, t * P:(t + 1) * P]
                    rest(gTlo[:, (c0 % 2) * 2:(c0 % 2) * 2 + 2, t * P:(t + 1) * P],
                         bank[:, 6 + t, 0:2 * P].rearrange("p (k n) -> p k n", k=2), o).then_inc(glo, 1)

                def pair(c, c0, i=0):
                    u = UB[f] + 2 + 3 * c0
                    split(l, u, i)
                    mul(c, 0)
                    rest_gu(c - 1, c0 - 1, 1)
                    split(l, u + 1, i)
                    mul(c, 1)
                    rest_gu(c, c0, 0)
                    split(l, u + 2, i)

                split(l, UB[f] + 2)
                mul(0, 0)
                split(l, UB[f] + 3)
                mul(0, 1)
                rest_gu(0, 0, 0)
                split(l, UB[f] + 4)
                with dve.Fori(0, (NCH - 3) // 2) as i:
                    pair(i * 2 + 1, 1, i * 2)
                    pair(i * 2 + 2, 2, i * 2)
                pair(NCH - 2, NCH - 2)
                c = NCH - 1
                if f == 0:
                    split(l, UB[f] + 2 + 3 * c)
                else:
                    split(l, UB[f] + U_FFN - 1)
                mul(c, 0)
                rest_gu(c - 1, c - 1, 1)
                if f == 0:
                    split(l, UB[f] + 3 + 3 * c)
                mul(c, 1)
                rest_gu(c, c, 0)
                if f == 0:
                    split(l, UB[f] + 4 + 3 * c)
                rest_gu(c, c, 1)

            def mixer(l):
                s = iter(range(UM + LEAD, UM + U_MIX + LEAD))
                done = [0]
                seen = {}

                def one():
                    split(l, next(s))

                def conv(ct, k):
                    if ct in seen:
                        dve.wait_ge(tap, l * N_TAP + seen[ct])
                    o = cacc[:, ct, :]
                    if k == W:
                        ins = nc.vector.tensor_scalar(o, o, 0.5, vec[:, V_CB + ct:V_CB + ct + 1], ALU.mult, ALU.add)
                    else:
                        i = cu[:, ct, k:k + SEQ]
                        w = vec[:, V_W + ct * W + k:V_W + ct * W + k + 1]
                        if k == 0:
                            ins = nc.vector.tensor_scalar(o, i, w, None, ALU.mult)
                        else:
                            ins = nc.vector.scalar_tensor_tensor(out=o, in0=i, scalar=w, in1=o, op0=ALU.mult,
                                                                 op1=ALU.add)
                    ins.then_inc(tap, 1)
                    done[0] += 1
                    seen[ct] = done[0]

                work = {ct: [(ct, k) for k in range(n)] for ct, n in ((3, D_TAPS), (0, W + 1), (2, W + 1))}
                turn = [0]

                def taps(n):
                    for _ in range(n):
                        now = [w for ct, w in work.items() if w and ct // 2 < len(ready)][:2]
                        if now:
                            conv(*now[turn[0] % len(now)].pop(0))
                            turn[0] += 1
                            if work[3] == [] and "tile 3" not in seen:
                                seen["tile 3"] = done[0]
                                assert done[0] == P_TAP

                ready = []

                def conv_gate(j, b0):
                    dve.wait_ge(tanh_ready, l * 2 + j + 1)
                    nc.vector.scalar_tensor_tensor(out=cu[:, 2 * j:2 * j + 2, W - 1:W - 1 + SEQ],
                                                   in0=cacc[:, 2 * j:2 * j + 2, :], scalar=1.0,
                                                   in1=bank[:, b0, :].rearrange("p (c n) -> p c n", c=2),
                                                   op0=ALU.add, op1=ALU.mult).then_inc(cu_ready, 1)
                    dve.wait_ge(cu_ready, l * 2 + j + 1)
                    ready.append(j)

                dve.wait_ge(pr_sq, (l + 1) * 4)
                nc.vector.tensor_scalar(ss4, ss4, 1.0 / QL, EPS, ALU.mult, ALU.add).then_inc(pr_ms, 1)
                dve.wait_ge(pr_rs, l + 1)
                lat = pr[:, :, 0:QL + KVL].rearrange("p t (j n) -> p t j n", j=2)
                nc.vector.tensor_tensor(lat, lat, rs4.rearrange("p (t j) -> p t j", t=2).unsqueeze(3)
                                        .to_broadcast([P, TT, 2, QL]), ALU.mult).then_inc(pr_norm, 1)
                one()
                dve.wait_ge(vec_landed, (l + 1) * 48)
                for j in range(2):
                    dve.wait_ge(lat_hi, l * 4 + 2 * j + 2)
                    for k in range(2):
                        nc.vector.scalar_tensor_tensor(out=gTlo[:, 2 * j + k, :],
                                                       in0=bank[:, 6 + j, k * SEQ:(k + 1) * SEQ],
                                                       scalar=vec[:, V_CQ + 2 * j + k:V_CQ + 2 * j + k + 1],
                                                       in1=gThi[:, 2 * j + k, :].bitcast(F32), op0=ALU.mult,
                                                       op1=ALU.subtract).then_inc(lat_lo, 1)
                one()
                conv_gate(0, 4)
                one()
                one()
                taps(EARLY_TAPS[0])
                one()
                tok = ktok[:, :, :, :]
                for j in range(2):
                    dve.wait_ge(qk_sq, l * 2 + j + 1)
                    sums = ssqk[:, 16 * j:16 * j + 16]
                    nc.vector.tensor_reduce(sums, junk.rearrange("p t (h d) -> p t h d", h=H), AX.X,
                                            ALU.add).then_inc(qk_sum, 1)
                    dve.wait_ge(qk_sum, l * 2 + j + 1)
                    nc.vector.tensor_scalar(sums, sums, 1.0 / QK, EPS, ALU.mult, ALU.add).then_inc(qk_ms, 1)
                    taps(EARLY_TAPS[1 + j])
                    if j:
                        dve.wait_ge(qk_rs, l * 2 + 2)
                        nc.vector.tensor_scalar(qscale, rsqk[:, 0:16], SCALE, None, ALU.mult).then_inc(qk_norm, 1)
                        dve.wait_ge(kr_ready, (l + 1) * 2)
                        r = rsqk[:, 16:32].rearrange("p (t h) -> p t h", t=TT).unsqueeze(3)
                        nc.vector.tensor_tensor(tok, tok, r.to_broadcast([P, TT, H, QK]), ALU.mult).then_inc(qk_norm, 1)
                    one()
                conv_gate(1, 0)

                def head_max(h):
                    dve.wait_ge(s_done, l * H + h + 1)
                    if h:
                        dve.wait_ge(pt_done, l * H + h)
                    nc.vector.memset(small[:, 94:95], 0.0)
                    nc.vector.tensor_tensor_reduce(out=prob[:, 0, 0:P], in0=bank[:, 5, 0:P], in1=mask[:, P:2 * P],
                                                   scale=1.0, scalar=-3e38, op0=ALU.add, op1=ALU.max,
                                                   accum_out=mx[:, 0:1]).then_inc(max_ready, 1)
                    nc.vector.tensor_tensor_reduce(out=prob[:, 1, :], in0=bank[:, 5, P:3 * P], in1=mask[:, :],
                                                   scale=1.0, scalar=-3e38, op0=ALU.add, op1=ALU.max,
                                                   accum_out=mx[:, 1:2]).then_inc(max_ready, 1)
                    dve.wait_ge(max_ready, l * (2 * H) + 2 * h + 2)
                    nc.vector.scalar_tensor_tensor(out=nmx, in0=mx, scalar=-1.0,
                                                   in1=qscale.rearrange("p (t h) -> p t h", t=TT)[:, :, h],
                                                   op0=ALU.mult, op1=ALU.mult).then_inc(nmx_ready, 1)

                def head_sum(h):
                    dve.wait_ge(exp_ready, l * H + h + 1)
                    nc.vector.reciprocal(rsum[h % 2], psum_h).then_inc(rsum_ready, 1)

                def head_out(h):
                    dve.wait_ge(pv_done, l * H + h + 1)
                    dve.wait_ge(rsum_ready, l * H + h + 1)
                    nc.vector.tensor_tensor(otok[:, :, h * VD:(h + 1) * VD], bank[:, 7, 0:2 * VD].rearrange("p (t d) -> p t d", t=TT),
                                            rsum[h % 2].unsqueeze(2).to_broadcast([P, TT, VD]),
                                            ALU.mult).then_inc(o_ready, 1)

                def gate_bias(g):
                    if g == 3:
                        dve.wait_ge(pool_tap, (l + 1) * N_PTAP)
                    for t in range(TT):
                        if t == 0:
                            dve.wait_ge(gate_done, l * 4 + g + 1)
                            dve.wait_ge(bias_landed, l * 64 + 16 * (g + 1))
                        else:
                            unit_released(dve, l, UM + M_G + 2 * g + 1)
                        nc.vector.tensor_tensor(gates[:, t, g * C:(g + 1) * C], bank[:, (2 if g % 2 == 0 else 0) + t, :],
                                                bias[:, :], ALU.add).then_inc(gate_sum, 1)

                for u8 in range(8):
                    if u8 == 1:
                        head_max(0)
                        one()
                        one()
                        head_max(1)
                        one()
                    taps(2 if u8 < 2 else 5)
                    if u8 % 2 == 0 and u8:
                        gate_bias(u8 // 2 - 1)
                    if u8 > 1:
                        one()
                    if u8 > 2:
                        head_max(u8 - 1)
                    if u8:
                        taps(4)
                    if u8 >= 2:
                        head_out(u8 - 2)
                    if u8 >= 1:
                        head_sum(u8 - 1)
                taps(CT * W)
                dve.wait_ge(pool_tap, (l + 1) * N_PTAP)
                for ct in (1, 3):
                    conv(ct, W)
                head_max(H - 1)
                head_out(H - 2)
                head_sum(H - 1)
                dve.wait_ge(mean_done, l + 1)
                nc.vector.tensor_tensor(cacc[:, :, :], cacc[:, :, :],
                                        bank[:, 3:4, 0:SEQ].to_broadcast([P, CT, SEQ]),
                                        ALU.subtract).then_inc(xc_ready, 1)
                head_out(H - 1)
                gate_bias(3)
                for t in range(TT):
                    dve.wait_ge(ot_hi, l * 2 + t + 1)
                    rest(hTlo[:, 0:4, t * P:(t + 1) * P], bank[:, 4 + t, :].rearrange("p (k n) -> p k n", k=4),
                         hThi[:, 0:4, t * P:(t + 1) * P]).then_inc(ot_lo, 1)
                assert done[0] == N_TAP

                def gated(t, half, b0, ready_sem):
                    o = gates[:, t, half * D:(half + 1) * D]
                    nc.vector.scalar_tensor_tensor(out=o, in0=o, scalar=1.0,
                                                   in1=bank[:, b0:b0 + 2, :].rearrange("p b n -> p (b n)"),
                                                   op0=ALU.add, op1=ALU.mult).then_inc(ready_sem, 1)

                dve.wait_ge(var_done, l + 1)
                nc.vector.tensor_scalar(ms, bank[:, 6, SEQ:SEQ + TT], EPS, None, ALU.add).then_inc(lnv_ready, 1)
                dve.wait_ge(lnr_ready, l + 1)
                for t in range(TT):
                    nc.vector.tensor_scalar(diag[:, t, :], ident[:, :], rs[:, t:t + 1], float(C), ALU.mult,
                                            ALU.mult).then_inc(diag_ready, 1)
                dve.wait_ge(lnb_done, l + 1)
                nc.vector.tensor_tensor(cacc[:, :, :], cacc[:, :, :],
                                        bank[:, 6:7, 0:SEQ].to_broadcast([P, CT, SEQ]),
                                        ALU.mult).then_inc(ln_ready, 1)
                one()
                dve.wait_ge(gate_ready, (l + 1) * 8)
                dve.wait_ge(mla_done, l + 1)
                gated(0, 1, 2, ym_ready)
                dve.wait_ge(c_hi, l + 1)
                rest(gTlo[:, :, :], cacc[:, :, :], gThi[:, :, :]).then_inc(c_lo, 1)
                nc.vector.memset(small[:, 90:91], 0.0).then_inc(vec_used, 1)
                unit_released(dve, l, UM + M_MLA + 1)
                gated(1, 1, 0, ym_ready)
                one()
                one()
                for t in range(TT):
                    if t == 0:
                        dve.wait_ge(co_done, l + 1)
                    else:
                        unit_released(dve, l, UM + M_CO + 1)
                    gated(t, 0, 4 + 2 * t, yc_ready)
                    dve.wait_ge(yc_ready, l * 2 + t + 1)
                    dve.wait_ge(ym_ready, l * 2 + 2)
                    for h in range(2):
                        o = gates[:, t, h * C:(h + 1) * C]
                        nc.vector.tensor_tensor(o, o, gates[:, t, D + h * C:D + (h + 1) * C],
                                                ALU.add).then_inc(y_ready, 1)
                    for h in range(2):
                        dve.wait_ge(yt_hi, l * 4 + t * 2 + h + 1)
                        rest(hTlo[:, 4 * h:4 * h + 4, t * P:(t + 1) * P],
                             bank[:, 2 * t + h, :].rearrange("p (k n) -> p k n", k=4),
                             hThi[:, 4 * h:4 * h + 4, t * P:(t + 1) * P]).then_inc(yt_lo, 1)
                    if t == 0:
                        one()
                        one()
                assert next(s) == UB[1] + 2

            nc.vector.memset(zero[:, :], 0.0).then_inc(dve_const, 1)
            nc.vector.memset(mask[:, :], 0.0).then_inc(dve_const, 1)
            nc.vector.memset(cu[:, :, 0:W - 1], 0.0)
            dve.wait_ge(dve_const, 2)
            nc.vector.memset(mask[0:CHUNK, P + CHUNK:2 * P], MASKED)
            dve.sem_inc(wlo_ready, RAW)
            dve.sem_inc(vec_used, 1)
            dve.sem_inc(h_ready, 1)
            dve.sem_inc(x_new, TT)

            with dve.Fori(0, DEPTH) as l:
                def norm(n, t):
                    norm_scale(l, n, t)
                    norm_apply(l, n, t)
                    norm_rest(l, n, t)

                for t in range(TT):
                    norm_scale(l, 0, t)
                    norm_apply(l, 0, t)
                    if t == 0:
                        split(l, 0)
                    norm_rest(l, 0, t)
                    if t == 0:
                        split(l, 1)
                ffn(l, 0)
                for t in range(TT):
                    residual(l, 0, t, 2 * t, UB[0] + U_FFN - 1)
                    norm(1, t)
                for u in range(UM + 2, UM + LEAD):
                    split(l, u)
                mixer(l)
                for t in range(TT):
                    residual(l, 1, t, 4 - 2 * t, UM + U_MIX - 1)
                    norm(2, t)
                ffn(l, 1)
                for t in range(TT):
                    residual(l, 2, t, 2 * t, UB[1] + U_FFN - 1)


_BIG = ["x", "positions", "ffn1_norm", "ffn1_w_gate", "ffn1_w_up", "ffn1_w_down", "mix_norm", "w_in", "gate_bias",
        "w_conv_out", "w_uq", "w_ukv", "q_norm", "k_norm", "w_mla_out", "w_out", "ffn2_norm", "ffn2_w_gate",
        "ffn2_w_up", "ffn2_w_down"]


def kernel(**inputs):
    import concourse.bacc as bacc
    from concourse.bass_utils import run_bass_kernel_spmd

    def tiles(v):
        return v.reshape(DEPTH, -1, P).transpose(0, 2, 1)

    arrays = {n: np.ascontiguousarray(inputs[n]) for n in _BIG}
    taps = np.asarray(inputs["conv_w"]).reshape(DEPTH, W, CT, P).transpose(0, 3, 2, 1).reshape(DEPTH, P, CT * W)
    ones = np.ones((DEPTH, P - NOPE), np.float32)
    qk = [np.concatenate([np.asarray(inputs[n])[:, :NOPE], ones], axis=1) for n in ("q_norm", "k_norm")]
    arrays["vec"] = np.ascontiguousarray(np.concatenate(
        [taps] + [tiles(np.asarray(inputs[n])) for n in ("conv_b", "conv_ln_g", "conv_ln_b", "cq_norm", "ckv_norm")]
        + [v[:, :, None] for v in qk],
        axis=2))
    nc = bacc.Bacc("TRN2", target_bir_lowering=False, num_devices=1, dynamic_dma_scratch_size=1024)
    args = {n: nc.dram_tensor(f"in_{n}", v.shape, mybir.dt.from_np(v.dtype), kind="ExternalInput").ap()
            for n, v in arrays.items()}
    args["out"] = nc.dram_tensor("out", (1, SEQ, D), F32, kind="ExternalOutput").ap()
    trunk(nc, args)
    r = run_bass_kernel_spmd(nc, [{f"in_{n}": v for n, v in arrays.items()}], core_ids=[0])
    return r.results[0]["out"]
```
